# Optimizing a Trainium2 kernel written in Bass

```python
import math
import jax, jax.numpy as jnp
from jax import lax
import numpy as np

D_MODEL = 1024
BATCH = 1
SEQ = 512
DEPTH = 1

PLE_DIM = 256
D_FF = 2816
EPS = 1e-6
MLA_HEADS = 8
MLA_Q_RANK = 256
MLA_KV_RANK = 256
MLA_NOPE = 64
MLA_ROPE = 32
MLA_V = 64
ROPE_THETA = 10000.0
Q_BLOCK = 128
ML_HEADS = 4
ML_QK = 64
ML_V = 128
ML_CHUNK = 128
CONV_W = 5
N_DIR = 2
MLA_OUT = MLA_HEADS * MLA_V
ML_OUT = ML_HEADS * ML_V
IN_SPLITS = (MLA_Q_RANK, MLA_KV_RANK, MLA_ROPE, ML_HEADS * ML_QK, ML_HEADS * ML_QK, ML_OUT,
             N_DIR * ML_HEADS, N_DIR * ML_HEADS, ML_OUT, 2 * D_MODEL)
IN_WIDTH = sum(IN_SPLITS)

kernel_name = 'hybrid_mla_mlstm_macaron_encoder'

def rmsnorm(x, w):
    xf = x.astype(jnp.float32)
    y = xf * lax.rsqrt(jnp.mean(xf * xf, axis=-1, keepdims=True) + EPS)
    return (y * w.astype(jnp.float32)).astype(x.dtype)

def swiglu(x, w_gate, w_up, w_down):
    return (jax.nn.silu(x @ w_gate) * (x @ w_up)) @ w_down

def apply_rope(x, cos, sin):
    half = x.shape[-1] // 2
    x1, x2 = x[..., :half], x[..., half:]
    return jnp.concatenate([x1 * cos - x2 * sin, x2 * cos + x1 * sin], axis=-1)

def depthwise_conv(x, w, b):
    C = x.shape[-1]
    y = lax.conv_general_dilated(x, w[:, None, :].astype(x.dtype), window_strides=(1,),
                                 padding=[(CONV_W // 2, CONV_W // 2)],
                                 dimension_numbers=('NWC', 'WIO', 'NWC'),
                                 feature_group_count=C)
    return y + b

def mla_branch(c_q, c_kv, k_r, cos, sin, q_norm, kv_norm, w_uq, w_uk, w_uv):
    B, S, _ = c_q.shape
    q = (rmsnorm(c_q, q_norm) @ w_uq).reshape(B, S, MLA_HEADS, MLA_NOPE + MLA_ROPE)
    q_nope = q[..., :MLA_NOPE]
    q_rope = apply_rope(q[..., MLA_NOPE:], cos[:, :, None, :], sin[:, :, None, :])
    ckv = rmsnorm(c_kv, kv_norm)
    k_nope = (ckv @ w_uk).reshape(B, S, MLA_HEADS, MLA_NOPE)
    v = (ckv @ w_uv).reshape(B, S, MLA_HEADS, MLA_V)
    k_rope = apply_rope(k_r, cos, sin)
    scale = (MLA_NOPE + MLA_ROPE) ** -0.5
    nb = S // Q_BLOCK
    qn_b = q_nope.reshape(B, nb, Q_BLOCK, MLA_HEADS, MLA_NOPE).transpose(1, 0, 2, 3, 4)
    qr_b = q_rope.reshape(B, nb, Q_BLOCK, MLA_HEADS, MLA_ROPE).transpose(1, 0, 2, 3, 4)

    def block(args):
        qn, qr = args
        s = (jnp.einsum('bqhd,bkhd->bhqk', qn, k_nope)
             + jnp.einsum('bqhd,bkd->bhqk', qr, k_rope))
        pr = jax.nn.softmax(s.astype(jnp.float32) * scale, axis=-1).astype(v.dtype)
        return jnp.einsum('bhqk,bkhd->bqhd', pr, v)

    o = lax.map(block, (qn_b, qr_b))
    return o.transpose(1, 0, 2, 3, 4).reshape(B, S, MLA_OUT)

def mlstm_chunkwise(q, k, v, li, lf):
    dtype = v.dtype
    q, k, v, li, lf = (t.astype(jnp.float32) for t in (q, k, v, li, lf))
    N, H, S, dk = q.shape
    dv = v.shape[-1]
    L = ML_CHUNK
    nc = S // L
    qc = q.reshape(N, H, nc, L, dk).transpose(2, 0, 1, 3, 4)
    kc = k.reshape(N, H, nc, L, dk).transpose(2, 0, 1, 3, 4)
    vc = v.reshape(N, H, nc, L, dv).transpose(2, 0, 1, 3, 4)
    ic = li.reshape(N, H, nc, L).transpose(2, 0, 1, 3)
    fc = lf.reshape(N, H, nc, L).transpose(2, 0, 1, 3)
    mask = jnp.tril(jnp.ones((L, L), dtype=bool))

    def step(carry, inp):
        C, n, m = carry
        qb, kb, vb, ib, fb = inp
        b = jnp.cumsum(fb, axis=-1)
        dmat = jnp.where(mask, b[..., :, None] - b[..., None, :] + ib[..., None, :], -jnp.inf)
        m_t = jnp.maximum(b + m[..., None], jnp.max(dmat, axis=-1))
        inter = jnp.exp(b + m[..., None] - m_t)
        s = jnp.einsum('nhtd,nhsd->nhts', qb, kb) * jnp.exp(dmat - m_t[..., None])
        num = (jnp.einsum('nhts,nhsv->nhtv', s, vb)
               + inter[..., None] * jnp.einsum('nhtd,nhdv->nhtv', qb, C))
        den = jnp.sum(s, axis=-1) + inter * jnp.einsum('nhtd,nhd->nht', qb, n)
        h = num / jnp.maximum(jnp.abs(den), jnp.exp(-m_t))[..., None]
        b_end = b[..., -1]
        g = b_end[..., None] - b + ib
        m_new = jnp.maximum(b_end + m, jnp.max(g, axis=-1))
        decay = jnp.exp(b_end + m - m_new)
        wgt = jnp.exp(g - m_new[..., None])
        C_new = decay[..., None, None] * C + jnp.einsum('nhs,nhsd,nhsv->nhdv', wgt, kb, vb)
        n_new = decay[..., None] * n + jnp.einsum('nhs,nhsd->nhd', wgt, kb)
        return (C_new, n_new, m_new), h

    init = (jnp.zeros((N, H, dk, dv), jnp.float32), jnp.zeros((N, H, dk), jnp.float32),
            jnp.zeros((N, H), jnp.float32))
    _, hs = lax.scan(step, init, (qc, kc, vc, ic, fc))
    return hs.transpose(1, 2, 0, 3, 4).reshape(N, H, S, dv).astype(dtype)

def mlstm_branch(ml_q, ml_k, ml_v, ml_i, ml_f, ml_o, conv_w, conv_b, i_bias, f_bias, head_norm):
    B, S, _ = ml_q.shape
    qk = jax.nn.silu(depthwise_conv(jnp.concatenate([ml_q, ml_k], axis=-1), conv_w, conv_b))
    q, k = jnp.split(qk, 2, axis=-1)
    q = q.reshape(B, S, ML_HEADS, ML_QK).transpose(0, 2, 1, 3)
    k = k.reshape(B, S, ML_HEADS, ML_QK).transpose(0, 2, 1, 3) * (ML_QK ** -0.5)
    v = ml_v.reshape(B, S, ML_HEADS, ML_V).transpose(0, 2, 1, 3)
    li = (ml_i.reshape(B, S, N_DIR, ML_HEADS) + i_bias).transpose(2, 0, 3, 1)
    lf = jax.nn.log_sigmoid(ml_f.reshape(B, S, N_DIR, ML_HEADS) + f_bias).transpose(2, 0, 3, 1)
    qd = jnp.stack([q, q[:, :, ::-1]]).reshape(N_DIR * B, ML_HEADS, S, ML_QK)
    kd = jnp.stack([k, k[:, :, ::-1]]).reshape(N_DIR * B, ML_HEADS, S, ML_QK)
    vd = jnp.stack([v, v[:, :, ::-1]]).reshape(N_DIR * B, ML_HEADS, S, ML_V)
    lid = jnp.stack([li[0], li[1][..., ::-1]]).reshape(N_DIR * B, ML_HEADS, S)
    lfd = jnp.stack([lf[0], lf[1][..., ::-1]]).reshape(N_DIR * B, ML_HEADS, S)
    hs = mlstm_chunkwise(qd, kd, vd, lid, lfd).reshape(N_DIR, B, ML_HEADS, S, ML_V)
    h = (hs[0] + hs[1][:, :, ::-1]).transpose(0, 2, 1, 3)
    h = rmsnorm(h, head_norm.reshape(ML_HEADS, ML_V)).reshape(B, S, ML_OUT)
    return h * jax.nn.sigmoid(ml_o)

def setup_inputs(seed: int = 0) -> dict:
    key = jax.random.key(seed)
    k = jax.random.split(key, 40)

    def w(kk, shape, fan_in):
        return jax.random.normal(kk, (DEPTH,) + shape, jnp.float32) * (fan_in ** -0.5)

    def gain(kk, n):
        return 1.0 + 0.05 * jax.random.normal(kk, (DEPTH, n), jnp.float32)

    x = jax.random.normal(k[0], (BATCH, SEQ, D_MODEL), jnp.float32)
    p = jax.random.normal(k[1], (DEPTH, BATCH, SEQ, PLE_DIM), jnp.float32)
    positions = (jnp.arange(SEQ, dtype=jnp.int32)[None, :]
                 + jax.random.randint(k[2], (BATCH, 1), 0, 1024, dtype=jnp.int32))
    return {
        'x': x, 'p': p, 'positions': positions,
        'ffn1_pre_norm': gain(k[3], D_MODEL), 'ffn1_post_norm': gain(k[4], D_MODEL),
        'ffn1_w_gate': w(k[5], (D_MODEL, D_FF), D_MODEL), 'ffn1_w_up': w(k[6], (D_MODEL, D_FF), D_MODEL),
        'ffn1_w_down': w(k[7], (D_FF, D_MODEL), D_FF),
        'mix_pre_norm': gain(k[8], D_MODEL), 'mix_post_norm': gain(k[9], D_MODEL),
        'w_in': w(k[10], (D_MODEL, IN_WIDTH), D_MODEL),
        'mla_q_norm': gain(k[11], MLA_Q_RANK), 'mla_kv_norm': gain(k[12], MLA_KV_RANK),
        'mla_w_uq': w(k[13], (MLA_Q_RANK, MLA_HEADS * (MLA_NOPE + MLA_ROPE)), MLA_Q_RANK),
        'mla_w_uk': w(k[14], (MLA_KV_RANK, MLA_HEADS * MLA_NOPE), MLA_KV_RANK),
        'mla_w_uv': w(k[15], (MLA_KV_RANK, MLA_HEADS * MLA_V), MLA_KV_RANK),
        'ml_conv_w': w(k[16], (CONV_W, 2 * ML_HEADS * ML_QK), CONV_W),
        'ml_conv_b': 0.02 * jax.random.normal(k[17], (DEPTH, 2 * ML_HEADS * ML_QK), jnp.float32),
        'ml_i_bias': -1.0 + 0.1 * jax.random.normal(k[18], (DEPTH, N_DIR, ML_HEADS), jnp.float32),
        'ml_f_bias': 3.0 + 0.5 * jax.random.normal(k[19], (DEPTH, N_DIR, ML_HEADS), jnp.float32),
        'ml_head_norm': gain(k[20], ML_OUT),
        'w_branch_mla': w(k[21], (MLA_OUT, D_MODEL), MLA_OUT),
        'w_branch_ml': w(k[22], (ML_OUT, D_MODEL), ML_OUT),
        'w_out': w(k[23], (D_MODEL, D_MODEL), D_MODEL),
        'ffn2_pre_norm': gain(k[24], D_MODEL), 'ffn2_post_norm': gain(k[25], D_MODEL),
        'ffn2_w_gate': w(k[26], (D_MODEL, D_FF), D_MODEL), 'ffn2_w_up': w(k[27], (D_MODEL, D_FF), D_MODEL),
        'ffn2_w_down': w(k[28], (D_FF, D_MODEL), D_FF),
        'ple_pre_norm': gain(k[29], D_MODEL), 'ple_post_norm': gain(k[30], D_MODEL),
        'ple_w_proj': w(k[31], (PLE_DIM, D_MODEL), PLE_DIM),
        'ple_w_gate': w(k[32], (D_MODEL, D_MODEL), D_MODEL),
    }

def reference(x, p, positions,
              ffn1_pre_norm, ffn1_post_norm, ffn1_w_gate, ffn1_w_up, ffn1_w_down,
              mix_pre_norm, mix_post_norm, w_in,
              mla_q_norm, mla_kv_norm, mla_w_uq, mla_w_uk, mla_w_uv,
              ml_conv_w, ml_conv_b, ml_i_bias, ml_f_bias, ml_head_norm,
              w_branch_mla, w_branch_ml, w_out,
              ffn2_pre_norm, ffn2_post_norm, ffn2_w_gate, ffn2_w_up, ffn2_w_down,
              ple_pre_norm, ple_post_norm, ple_w_proj, ple_w_gate):
    inv_freq = ROPE_THETA ** (-jnp.arange(0, MLA_ROPE, 2, dtype=jnp.float32) / MLA_ROPE)
    ang = positions.astype(jnp.float32)[..., None] * inv_freq
    cos = jnp.cos(ang).astype(x.dtype)
    sin = jnp.sin(ang).astype(x.dtype)
    split_idx = [int(s) for s in np.cumsum(IN_SPLITS)[:-1]]

    h = x
    for i in range(DEPTH):
        u = rmsnorm(h, ffn1_pre_norm[i])
        h = h + 0.5 * rmsnorm(swiglu(u, ffn1_w_gate[i], ffn1_w_up[i], ffn1_w_down[i]), ffn1_post_norm[i])

        u = rmsnorm(h, mix_pre_norm[i])
        z = u @ w_in[i]
        c_q, c_kv, k_r, ml_q, ml_k, ml_v, ml_i, ml_f, ml_o, gates = jnp.split(z, split_idx, axis=-1)
        a = mla_branch(c_q, c_kv, k_r, cos, sin, mla_q_norm[i], mla_kv_norm[i],
                       mla_w_uq[i], mla_w_uk[i], mla_w_uv[i]) @ w_branch_mla[i]
        bm = mlstm_branch(ml_q, ml_k, ml_v, ml_i, ml_f, ml_o, ml_conv_w[i], ml_conv_b[i],
                          ml_i_bias[i], ml_f_bias[i], ml_head_norm[i]) @ w_branch_ml[i]
        g_a, g_b = jnp.split(jax.nn.sigmoid(gates), 2, axis=-1)
        mixed = (g_a * a + g_b * bm) @ w_out[i]
        h = h + rmsnorm(mixed, mix_post_norm[i])

        u = rmsnorm(h, ffn2_pre_norm[i])
        h = h + 0.5 * rmsnorm(swiglu(u, ffn2_w_gate[i], ffn2_w_up[i], ffn2_w_down[i]), ffn2_post_norm[i])

        e = p[i] @ ple_w_proj[i]
        g = jax.nn.sigmoid(rmsnorm(h, ple_pre_norm[i]) @ ple_w_gate[i])
        h = h + rmsnorm(g * e, ple_post_norm[i])
    return h


_drawn_inputs = setup_inputs


def setup_inputs(seed=0):
    import zlib

    import numpy as np

    out = dict(_drawn_inputs(seed))
    spreads = {}
    factors = {'mla_q_norm': 8.0,
     'mla_kv_norm': 7.559,
     'ml_conv_b': 30.392,
     'ml_i_bias': 13.501,
     'ffn2_pre_norm': 2.891,
     'ffn2_post_norm': 4.064,
     'ple_pre_norm': 19.621,
     'ml_f_bias': 30.008,
     'ml_head_norm': 64.0,
     'ple_post_norm': 3.015}
    for name, (base, spread) in spreads.items():
        noise = np.random.default_rng([zlib.crc32(name.encode()), seed]).standard_normal(out[name].shape)
        drawn = base * np.exp(spread * noise) if base else spread * noise
        out[name] = __import__('jax').numpy.asarray(drawn.astype(out[name].dtype))
    for name, factor in factors.items():
        out[name] = (out[name] * factor).astype(out[name].dtype)
    return out
```

```python
from contextlib import ExitStack
import numpy as np
import concourse.bass as bass
from concourse import mybir

ALU = mybir.AluOpType
ACT = mybir.ActivationFunctionType
AX = mybir.AxisListType
F32 = mybir.dt.float32
F32R = mybir.dt.float32r
I32 = mybir.dt.int32

P = 128
S = 512
D = 1024
KD = D // P
TB = S // P
F = 2816
KF = F // P
PLE = 256
EPS = 1e-6
RANK = 256
HEADS, NOPE, ROPE, VDIM = 8, 64, 32, 64
MLH, MLQK, MLV = 4, 64, 128
CONV = 5
BIG = 1e30
SCALE = float((NOPE + ROPE) ** -0.5)
RING = 4
CH = 1024

C_KV, C_KR = RANK, 2 * RANK
C_MQ = C_KR + ROPE
C_MK = C_MQ + MLH * MLQK
C_MV = C_MK + MLH * MLQK
C_I = C_MV + MLH * MLV
C_F = C_I + 2 * MLH
C_MO = C_F + 2 * MLH
C_G = C_MO + MLH * MLV

UP1 = 0
UPN = 4 * (F // 256)
DN1 = UP1 + UPN
CQ = DN1 + KF
SPC = CQ + 4
MQK = SPC + 1
UQ = MQK + 4
UK = UQ + 2
UV = UK + 1
GAC = UV + 1
MV = GAC + 8
MO = MV + 4
GBC = MO + 4
BA = GBC + 8
BB = BA + 4
WO = BB + 4
UP2 = WO + 8
DN2 = UP2 + UPN
EP = DN2 + KF
PG = EP + 2
CHUNKS = PG + 8

VEC_ROWS = [("ffn1_pre_norm", 8), ("ffn1_post_norm", 8), ("mix_pre_norm", 8), ("mix_post_norm", 8),
            ("ffn2_pre_norm", 8), ("ffn2_post_norm", 8), ("ple_pre_norm", 8), ("ple_post_norm", 8),
            ("mla_q_norm", 2), ("mla_kv_norm", 2), ("ml_conv_b", 4), ("ml_conv_w", 4 * CONV),
            ("ml_head_norm", 4)]
VEC = {}
NVEC = 0
for _name, _rows in VEC_ROWS:
    VEC[_name] = NVEC
    NVEC += _rows

YBANK = [4, 5, 6, 7, 0, 1, 2, 3]
R1_BANK, HSTAT_BANK, R2_BANK = 0, 2, 3


def loaded_totals():
    dmas = {SPC: 5, UQ: 6, UQ + 1: 6}
    slot, out = [0] * RING, []
    for n in range(CHUNKS):
        slot[n % RING] += 16 * dmas.get(n, 1)
        out.append(slot[n % RING])
    return out


LOADED = loaded_totals()


def program(nc, w, const, out):
    ctx = ExitStack()
    with ctx:
        block_build(nc, w, const, out, ctx)


def block_build(nc, w, const, out, ctx):
    cursor = [(nc.sbuf_base + 63) // 64 * 64]

    def at(name, shape, dt, offset):
        return nc.alloc_sbuf_tensor_at(name, shape, dt, offset=offset)

    def sb(name, shape, dt=F32):
        n = int(np.prod(shape[1:])) * 4
        t = at(name, shape, dt, cursor[0])
        cursor[0] += (n + 31) // 32 * 32
        return t

    h = sb("h", [P, KD, S])
    v_hi = sb("v_hi", [P, KD, S], F32R)
    v_lo = sb("v_lo", [P, KD, S], F32R)
    w_raw = sb("w_raw", [P, RING, CH])
    w_hi = sb("w_hi", [P, RING, CH], F32R)
    w_lo = sb("w_lo", [P, RING, CH], F32R)
    ident = sb("ident", [P, P])
    ones = sb("ones", [P, P])
    cols = sb("cols", [P, NVEC])
    r_b = sb("r_b", [P, S])
    sqacc = sb("sqacc", [P, S])
    scratch = sb("scratch", [P, 4, S])
    small = sb("small", [P, 320])
    A0 = cursor[0]
    KB = 1024
    assert A0 + 97 * KB <= nc.sbuf_usable_end, (A0, nc.sbuf_usable_end)

    def ar(name, shape, kb, dt=F32):
        return at(name, shape, dt, A0 + int(kb * KB))

    prod_hi = ar("prod_hi", [P, KF, S], 0, F32R)
    prod_lo = ar("prod_lo", [P, KF, S], 44, F32R)
    ys = ar("ys", [P, KD, S], 0)
    tbuf = ar("tbuf", [P, 2, S], 90)
    x_tm = ar("x_tm", [P, TB, D], 0)
    vec_rows = ar("vec_rows", [P, P], 20)
    pos_i = ar("pos_i", [P, S], 24, I32)
    ang = ar("ang", [P, S], 26)
    turns = ar("turns", [P, S], 28)
    trig = ar("trig", [P, 4], 96.5)
    CS = ar("CS", [P, S], 88)
    gates_a = ar("gates_a", [P, 8, S], 0)
    cq_t = ar("cq_t", [P, 4, S], 0)
    conv_in = ar("conv_in", [P, 4, S + 4], 8)
    Q = ar("Q", [P, HEADS, S], 16.5)
    K = ar("K", [P, HEADS, S], 32.5)
    Vm = ar("Vm", [P, TB, S], 48.5)
    cq_hi = ar("cq_hi", [P, 4, S], 56.5, F32R)
    cq_lo = ar("cq_lo", [P, 4, S], 64.5, F32R)
    Pm = ar("Pm", [P, TB, S], 56.5)
    O = ar("O", [P, TB, S], 64.5)
    PT = ar("PT", [P, 2, S], 72.5)
    mqk = ar("mqk", [P, 4, S], 76.5)
    lf_row = tbuf[0:8, 0, :]
    i_row = tbuf[0:8, 1, :]
    oT_hi = ar("oT_hi", [P, 4, S], 16.5, F32R)
    oT_lo = ar("oT_lo", [P, 4, S], 24.5, F32R)
    gates_b = ar("gates_b", [P, 8, S], 32.5)
    V = ar("V", [P, TB, S], 48.5)
    og = ar("og", [P, TB, S], 56.5)
    HS = ar("HS", [P, TB, S], 64.5)
    K_tm = ar("K_tm", [P, TB, 256], 72.5)
    C = ar("C", [P, 2, 2, P], 84.5)
    maskbig = ar("maskbig", [P, 2, P], 86.5)
    Mrows = ar("Mrows", [P, S], 88)
    hn_junk = ar("hn_junk", [P, S], 94)
    bT_hi = ar("bT_hi", [P, 4, S], 48.5, F32R)
    bT_lo = ar("bT_lo", [P, 4, S], 76.5, F32R)
    cx = ar("cx", [P, 2, TB, 4, 8], 96)
    e_sb = ar("e_sb", [P, KD, S], 20)
    p_tm = [ar("p_tm0", [P, 2, PLE], 88), ar("p_tm1", [P, 2, PLE], 94)]
    pT_hi = ar("pT_hi", [P, 2, S], 40, F32R)
    pT_lo = ar("pT_lo", [P, 2, S], 44, F32R)
    o_sb = ar("o_sb", [P, TB, D], 50)

    B = [ctx.enter_context(nc.psum_tensor(f"bank{i}", [P, S], F32)) for i in range(8)]

    used = [0]

    def scol(n):
        a = used[0]
        used[0] += n
        assert used[0] <= 320
        return small[:, a:a + n]

    nw = [scol(16) for _ in range(4)]
    r1c = scol(4)
    rc = scol(4)
    rq = scol(8)
    rqs = scol(4)
    mx = scol(4)
    nb = scol(4)
    sums = scol(32)
    rsum = scol(4)
    halfpost = scol(16)
    nstate = scol(4)
    decb = scol(16)
    den = scol(8)
    hsq = scol(16)
    hrs = scol(16)
    ifb = scol(2)
    mc = [scol(4), scol(4)]
    dcy = [scol(4), scol(4)]
    D8 = [scol(32), scol(32)]

    def sem(name):
        return ctx.enter_context(nc.semaphore(name))

    w_loaded = [sem(f"w_loaded{s}") for s in range(RING)]
    w_hi_done, w_lo_done, w_used = sem("w_hi_done"), sem("w_lo_done"), sem("w_used")
    consts_in, x_in, p_in, pos_in = sem("consts_in"), sem("x_in"), sem("p_in"), sem("pos_in")
    masks_made = sem("masks_made")
    pool_step, dve_step, act_step = sem("pool_step"), sem("dve_step"), sem("act_step")
    ones_made, vecs_T, cols_ready = sem("ones_made"), sem("vecs_T"), sem("cols_ready")
    ang_ready, cs_ready = sem("ang_ready"), sem("cs_ready")
    out_stored = sem("out_stored")

    class Signals(dict):
        def __init__(self, prefix):
            super().__init__()
            self.prefix = prefix

        def __missing__(self, name):
            self[name] = sem(f"{self.prefix}_{name}")
            return self[name]

    class Boundary:
        signals = Signals("boundary")
        PER = {"y_ready": (8, 7, 0, 7, 0), "ysq_dve": (0, 4, 4, 4, 0), "ysq_act": (0, 4, 4, 4, 8),
               "y_sum": (0, 8, 8, 8, 8), "r1_ready": (0, 1, 1, 1, 1), "r1b_ready": (0, 1, 1, 1, 1),
               "h_ready": (8,) * 5, "vhi_ready": (8,) * 5, "v_ready": (8,) * 5, "hsq_ready": (8,) * 5,
               "h_acc": (8,) * 5, "h2_ready": (1,) * 5, "r2_ready": (1,) * 5, "r2b_ready": (1,) * 5,
               "rb_ready": (1,) * 5}

        def __init__(self, n):
            self.n = n

        def __getitem__(self, name):
            return self.signals[name]

        def wait(self, eng, name, value):
            eng.wait_ge(self.signals[name], sum(self.PER[name][:self.n]) + value)

    bs = [Boundary(n) for n in range(5)]

    def three(o, ws, a_hi, a_lo, start, stop):
        whi, wlo = ws
        nc.tensor.matmul(o, whi, a_hi, start=start, stop=False)
        nc.tensor.matmul(o, whi, a_lo, start=False, stop=False)
        return nc.tensor.matmul(o, wlo, a_hi, start=False, stop=stop)

    def three_tm(o, ws, a_hi, a_lo, start, stop):
        whi, wlo = ws
        nc.tensor.matmul(o, a_hi, whi, start=start, stop=False)
        nc.tensor.matmul(o, a_hi, wlo, start=False, stop=False)
        return nc.tensor.matmul(o, a_lo, whi, start=False, stop=stop)

    def wv(n, a, b):
        s = n % RING
        return w_hi[:, s, a:b], w_lo[:, s, a:b]

    def split_hi(act, n, it=0):
        if n >= CHUNKS:
            return
        s = n % RING
        act.wait_ge(w_loaded[s], LOADED[n] + 16 * it)
        if n >= RING or not isinstance(it, int):
            act.wait_ge(w_used, n - RING + 1 + 4 * it)
        nc.scalar.activation(w_hi[:, s, :], w_raw[:, s, :], ACT.Copy).then_inc(w_hi_done, 1)

    def split_lo(dve, n, it=0):
        if n >= CHUNKS:
            return
        s = n % RING
        dve.wait_ge(w_hi_done, n + 1 + 4 * it)
        nc.vector.tensor_tensor(w_lo[:, s, :], w_raw[:, s, :], w_hi[:, s, :].bitcast(F32),
                                ALU.subtract).then_inc(w_lo_done, 1)

    hi_next, lo_next = [0], [0]

    def hi_upto(act, n):
        while hi_next[0] <= min(n, CHUNKS - 1):
            split_hi(act, hi_next[0])
            hi_next[0] += 1

    def lo_upto(dve, n):
        while lo_next[0] <= min(n, CHUNKS - 1):
            split_lo(dve, lo_next[0])
            lo_next[0] += 1

    def act_after(act, n):
        hi_upto(act, n + 3)
        act.wait_ge(w_used, n + 1)

    def dve_after(dve, n):
        lo_upto(dve, n + 3)
        dve.wait_ge(w_used, n + 1)

    dn, an, pn = [0], [0], [0]

    def dlink(dve, ins):
        dn[0] += 1
        ins.then_inc(dve_step, 1)
        dve.wait_ge(dve_step, dn[0])

    def alink(act, ins):
        an[0] += 1
        ins.then_inc(act_step, 1)
        act.wait_ge(act_step, an[0])

    def plink(pool, ins):
        pn[0] += 1
        ins.then_inc(pool_step, 1)
        pool.wait_ge(pool_step, pn[0])

    def rsqrt(dve, dst, src, n, inv):
        x, y, t, u = (a[:, 0:n] for a in nw)
        dlink(dve, nc.vector.tensor_scalar(x, src, inv, EPS, ALU.mult, ALU.add))
        dlink(dve, nc.vector.tensor_scalar(t.bitcast(I32), x.bitcast(I32), 1, None, ALU.logical_shift_right))
        dlink(dve, nc.vector.tensor_scalar(y.bitcast(I32), t.bitcast(I32), -1.0, float(0x5F3759DF),
                                           ALU.mult, ALU.add))
        for k in range(3):
            dlink(dve, nc.vector.scalar_tensor_tensor(t, y, -0.5, y, ALU.mult, ALU.mult))
            dlink(dve, nc.vector.tensor_tensor(u, t, x, ALU.mult))
            last = nc.vector.scalar_tensor_tensor(dst if k == 2 else y, u, 1.5, y, ALU.add, ALU.mult)
            if k < 2:
                dlink(dve, last)
        return last

    def col(name, m):
        c = VEC[name] + m
        return cols[:, c:c + 1]

    def bcast_rows(o, c, last_only=True):
        for tb in range(TB):
            last = nc.tensor.matmul(o[:, tb * P:(tb + 1) * P], c[:, tb:tb + 1].broadcast_to([P, P]), ident[:],
                                    start=True, stop=True)
        return last

    def token_sums(o, src):
        for tb in range(TB):
            last = nc.tensor.matmul(o[:, tb:tb + 1], src[:, tb * P:(tb + 1) * P], ones[:, 0:1], start=True, stop=True)
        return last

    def boundary_pe(pe, n, filler=None):
        b = bs[n]
        for p in range(KD):
            b.wait(pe, "ysq_act" if p % 2 == 0 else "ysq_dve", p // 2 + 1)
            for tb in range(TB):
                last = nc.tensor.matmul(B[YBANK[0]][:, tb:tb + 1], scratch[:, p % 4, tb * P:(tb + 1) * P],
                                        ones[:, 0:1], start=(p == 0 and tb == 0), stop=(p == KD - 1),
                                        skip_group_check=True)
            last.then_inc(b["y_sum"], 1)
        if filler:
            filler(0)
        b.wait(pe, "r1_ready", 1)
        bcast_rows(B[R1_BANK], r1c).then_inc(b["r1b_ready"], 1)
        if filler:
            filler(1)

    def y_tile(n, dve_side, eng, p, ready, src):
        b = bs[n]
        ready(eng, p)
        if p >= 4:
            b.wait(eng, "y_sum", p - 3)
        if dve_side:
            dlink(eng, nc.vector.tensor_copy(ys[:, p, :], src(p)))
            nc.vector.tensor_tensor(scratch[:, p % 4, :], ys[:, p, :], ys[:, p, :], ALU.mult).then_inc(b["ysq_dve"], 1)
        else:
            alink(eng, nc.scalar.activation(ys[:, p, :], src(p), ACT.Copy))
            nc.scalar.activation(scratch[:, p % 4, :], ys[:, p, :], ACT.Square).then_inc(b["ysq_act"], 1)

    def post_norm_dve(dve, n, post):
        b = bs[n]
        b.wait(dve, "y_sum", KD)
        rsqrt(dve, r1c, B[YBANK[0]][:, 0:TB], TB, 1.0 / D).then_inc(b["r1_ready"], 1)
        b.wait(dve, "r1b_ready", 1)

    def h_tile_dve(dve, n, m, post):
        b = bs[n]
        t = tbuf[:, m % 2, :]
        dlink(dve, nc.vector.scalar_tensor_tensor(t, ys[:, m, :], post(m), B[R1_BANK][:], ALU.mult, ALU.mult))
        nc.vector.tensor_tensor(h[:, m, :], h[:, m, :], t, ALU.add).then_inc(b["h_ready"], 1)

    def v_lo_dve(dve, n, m, pre):
        b = bs[n]
        b.wait(dve, "vhi_ready", m + 1)
        b.wait(dve, "h_ready", m + 1)
        nc.vector.scalar_tensor_tensor(v_lo[:, m, :], h[:, m, :], pre(m), v_hi[:, m, :].bitcast(F32),
                                       ALU.mult, ALU.subtract).then_inc(b["v_ready"], 1)

    def boundary_dve(dve, n, post, pre):
        post_norm_dve(dve, n, post)
        for m in range(KD):
            h_tile_dve(dve, n, m, post)
            if m >= 1:
                v_lo_dve(dve, n, m - 1, pre)
        v_lo_dve(dve, n, KD - 1, pre)

    def v_tiles_act(act, n, pre):
        b = bs[n]
        for m in range(KD):
            b.wait(act, "h_ready", m + 1)
            nc.scalar.activation(v_hi[:, m, :], h[:, m, :], ACT.Copy, scale=pre(m)).then_inc(b["vhi_ready"], 1)
            if m >= 4:
                b.wait(act, "h_acc", m - 3)
            nc.scalar.activation(scratch[:, m % 4, :], h[:, m, :], ACT.Square).then_inc(b["hsq_ready"], 1)

    def h_squares_pool(pool, n):
        b = bs[n]
        for m in range(KD):
            b.wait(pool, "hsq_ready", m + 1)
            if m == 0:
                nc.gpsimd.tensor_copy(sqacc[:], scratch[:, 0, :]).then_inc(b["h_acc"], 1)
            else:
                b.wait(pool, "h_acc", m)
                nc.gpsimd.tensor_tensor(sqacc[:], sqacc[:], scratch[:, m % 4, :], ALU.add).then_inc(b["h_acc"], 1)

    def lead_pe(pe, n, N):
        b = bs[n]
        for j in range(4):
            pe.wait_ge(w_lo_done, N + j + 1)
            for kk in range(4):
                k = 4 * (j // 2) + kk
                if j % 2 == 0:
                    b.wait(pe, "v_ready", max(k + 1, 2))
                for f in range(2):
                    c = kk * 256 + f * P
                    last = three(B[4 + 2 * (j % 2) + f][:], wv(N + j, c, c + P), v_hi[:, k, :], v_lo[:, k, :],
                                 k == 0, k == KD - 1)
            last.then_inc(w_used, 1)
            if j == 2:
                b.wait(pe, "h_acc", KD)
                token_sums(B[HSTAT_BANK], sqacc).then_inc(b["h2_ready"], 1)
        b.wait(pe, "r2_ready", 1)
        bcast_rows(B[R2_BANK], rc).then_inc(b["r2b_ready"], 1)

    def lead_dve(dve, n, N):
        b = bs[n]
        lo_upto(dve, N + 4)
        b.wait(dve, "h2_ready", 1)
        rsqrt(dve, rc, B[HSTAT_BANK][:, 0:TB], TB, 1.0 / D).then_inc(b["r2_ready"], 1)
        lo_upto(dve, N + 5)
        b.wait(dve, "r2b_ready", 1)
        nc.vector.tensor_copy(r_b[:], B[R2_BANK][:]).then_inc(b["rb_ready"], 1)
        b.wait(dve, "rb_ready", 1)

    def lead_act(act, n, N):
        hi_upto(act, N + 5)

    def ffn(n, N, DN, wg, wu, wd):
        gate0, silu0 = sem(f"f{n}_gate0"), sem(f"f{n}_silu0")
        gate_scaled, silu_done = sem(f"f{n}_gate_scaled"), sem(f"f{n}_silu_done")
        silu_r, prod_done = sem(f"f{n}_silu_r"), sem(f"f{n}_prod_done")
        phi, prod_ready = sem(f"f{n}_phi"), sem(f"f{n}_prod_ready")
        NI = F // 256
        yb = bs[n + 1]

        def sp_load(sp, i, j):
            m = N + j
            up, half = (j // 2, j % 2) if not isinstance(i, int) else (j % 2, j // 2)
            src = (wu if up else wg)[0, half * 512:half * 512 + 512, bass.ds(i * 256, 256)]
            sp.dma_start(w_raw[:, m % RING, :].rearrange("p (k c) -> p k c", k=4),
                         src.rearrange("(k p) c -> p k c", p=P)).then_inc(w_loaded[m % RING], 16)

        def sp_prog(sp):
            for j in range(4):
                if N + j >= RING:
                    sp.wait_ge(w_lo_done, N + j - RING + 1)
                sp_load(sp, 0, j)
            with sp.Fori(1, NI) as i:
                for j in range(4):
                    sp.wait_ge(w_lo_done, 4 * i + (N + j - RING + 1))
                    sp_load(sp, i, j)
            def down(k, j):
                m = DN + j
                sp.wait_ge(w_lo_done, k + (DN - RING + 1))
                sp.dma_start(w_raw[:, m % RING, :], wd[0, bass.ds(k * P, P), :]).then_inc(w_loaded[m % RING], 16)
            with sp.Fori(0, KF // 4) as i:
                for j in range(4):
                    down(4 * i + j, j)
            for j in range(KF // 4 * 4, KF):
                down(j, j)

        def pe_prog(pe):
            lead_pe(pe, n, N)
            with pe.Fori(1, NI) as i:
                for j in range(4):
                    pe.wait_ge(w_lo_done, 4 * i + (N + j + 1))
                    if j == 0:
                        pe.wait_ge(gate_scaled, 2 * i)
                    if j == 2:
                        pe.wait_ge(prod_done, 2 * i)
                    for kk in range(4):
                        k = 4 * (j % 2) + kk
                        for f in range(2):
                            c = kk * 256 + f * P
                            last = three(B[2 * (j // 2) + f][:], wv(N + j, c, c + P), v_hi[:, k, :], v_lo[:, k, :],
                                         k == 0, k == KD - 1)
                    last.then_inc(w_used, 1)

            def down(k, j, first=False, final=False):
                pe.wait_ge(w_lo_done, k + (DN + 1))
                ph = prod_hi[:, k, :] if isinstance(k, int) else prod_hi[:, bass.ds(k, 1), :].rearrange("p a s -> p (a s)")
                pl = prod_lo[:, k, :] if isinstance(k, int) else prod_lo[:, bass.ds(k, 1), :].rearrange("p a s -> p (a s)")
                for m in range(KD):
                    if first and m == 4:
                        pe.wait_ge(gate_scaled, 2 * NI)
                    if first and m == 6:
                        pe.wait_ge(prod_done, 2 * NI)
                    last = three(B[YBANK[m]][:], wv(DN + j, m * P, (m + 1) * P), ph, pl, first, final)
                    if final and m < KD - 1:
                        last.then_inc(yb["y_ready"], 1)
                last.then_inc(w_used, 1)

            pe.wait_ge(prod_ready, 2 * (NI - 1))
            for k in range(4):
                down(k, k, first=(k == 0))
            with pe.Fori(1, KF // 4) as i:
                for j in range(4):
                    down(4 * i + j, j)
            pe.wait_ge(prod_ready, 2 * NI)
            for k in range(KF // 4 * 4, KF):
                down(k, k, final=(k == KF - 1))

        def gates_dve(dve, i, first):
            for f in range(2):
                dve.wait_ge(w_used, 4 * i + (N + (3 if first else 2)))
                if not first:
                    dve.wait_ge(prod_ready, 2 * i + f - 1)
                nc.vector.tensor_tensor(scratch[:, f, :], B[(4 if first else 0) + f][:], r_b[:],
                                        ALU.mult).then_inc(gate0 if first else gate_scaled, 1)
            for f in range(2):
                dve.wait_ge(silu0 if first else silu_done, (f + 1) if first else 2 * i + (f - 1))
                nc.vector.tensor_tensor(scratch[:, f, :], scratch[:, f, :], r_b[:], ALU.mult).then_inc(silu_r, 1)

        def ups_dve(dve, i, first):
            dve.wait_ge(w_used, 4 * i + (N + 4))
            for f in range(2):
                dve.wait_ge(silu_r, 2 * i + (f + 1))
                if not first:
                    dve.wait_ge(phi, 2 * i + (f - 1))
                nc.vector.tensor_tensor(scratch[:, 2 + f, :], B[(6 if first else 2) + f][:], scratch[:, f, :],
                                        ALU.mult).then_inc(prod_done, 1)
            for f in range(2):
                dve.wait_ge(phi, 2 * i + (f + 1))
                o = prod_lo[:, 2 * i + f, :] if first else prod_lo[:, bass.ds(2 * i + f, 1), :].rearrange("p a s -> p (a s)")
                hh = prod_hi[:, 2 * i + f, :] if first else prod_hi[:, bass.ds(2 * i + f, 1), :].rearrange("p a s -> p (a s)")
                nc.vector.tensor_tensor(o, scratch[:, 2 + f, :], hh.bitcast(F32), ALU.subtract).then_inc(prod_ready, 1)

        def dve_prog(dve):
            dve.sem_inc(gate_scaled, 2)
            lead_dve(dve, n, N)
            gates_dve(dve, 0, True)
            lo_upto(dve, N + 6)
            ups_dve(dve, 0, True)
            assert lo_next[0] == N + 7
            with dve.Fori(1, NI) as i:
                for j in range(3):
                    split_lo(dve, N + 3 + j, i)
                gates_dve(dve, i, False)
                split_lo(dve, N + 6, i)
                ups_dve(dve, i, False)
            with dve.Fori(0, KF // 4) as i:
                for j in range(4):
                    split_lo(dve, DN + 3 + j, i)
            lo_next[0] = DN + 3 + KF // 4 * 4
            lo_upto(dve, DN + KF + 2)

        def silu_act(act, i, first):
            for f in range(2):
                act.wait_ge(gate0 if first else gate_scaled, (f + 1) if first else 2 * i + (f + 1))
                nc.scalar.activation(scratch[:, f, :], scratch[:, f, :], ACT.Silu).then_inc(silu0 if first else silu_done, 1)

        def phi_act(act, i, first):
            for f in range(2):
                act.wait_ge(prod_done, 2 * i + (f + 1))
                o = prod_hi[:, 2 * i + f, :] if first else prod_hi[:, bass.ds(2 * i + f, 1), :].rearrange("p a s -> p (a s)")
                nc.scalar.activation(o, scratch[:, 2 + f, :], ACT.Copy).then_inc(phi, 1)

        def act_prog(act):
            lead_act(act, n, N)
            silu_act(act, 0, True)
            hi_upto(act, N + 6)
            phi_act(act, 0, True)
            with act.Fori(1, NI) as i:
                for j in range(3):
                    split_hi(act, N + 3 + j, i)
                silu_act(act, i, False)
                split_hi(act, N + 6, i)
                phi_act(act, i, False)
            with act.Fori(0, KF // 4) as i:
                for j in range(4):
                    split_hi(act, DN + 3 + j, i)
            hi_next[0] = DN + 3 + KF // 4 * 4
            hi_upto(act, DN + KF + 2)

        def y_wait(eng, p):
            if p < KD - 1:
                yb.wait(eng, "y_ready", p + 1)
            else:
                eng.wait_ge(w_used, DN + KF)

        return sp_prog, pe_prog, dve_prog, act_prog, y_wait

    f1 = ffn(0, UP1, DN1, w["ffn1_w_gate"], w["ffn1_w_up"], w["ffn1_w_down"])
    f2 = ffn(2, UP2, DN2, w["ffn2_w_gate"], w["ffn2_w_up"], w["ffn2_w_down"])

    def half_post(a):
        return lambda m: halfpost[:, 8 * a + m:8 * a + m + 1]

    def gain(name):
        return lambda m: col(name, m)

    def ybank(p):
        return B[YBANK[p]][:]

    ms = Signals("mix")

    w_in = w["w_in"]

    def sp_chunk(sp, n, pieces):
        if n >= RING:
            sp.wait_ge(w_lo_done, n - RING + 1)
        for dst, src in pieces:
            sp.dma_start(dst, src).then_inc(w_loaded[n % RING], 16)

    def raw(n):
        return w_raw[:, n % RING, :]

    def cols4(sp, n, wt, half, c0):
        sp_chunk(sp, n, [(raw(n).rearrange("p (k c) -> p k c", k=4),
                          wt[0, half * 512:half * 512 + 512, c0:c0 + 256].rearrange("(k p) c -> p k c", p=P))])

    def cols2(sp, n, wt, r0, c0):
        sp_chunk(sp, n, [(raw(n).rearrange("p (k c) -> p k c", k=2),
                          wt[0, r0:r0 + 256, c0:c0 + 512].rearrange("(k p) c -> p k c", p=P))])

    def mixer_sp(sp):
        for j in range(4):
            cols4(sp, CQ + j, w_in, j // 2, 256 * (j % 2))
        r = raw(SPC).rearrange("p (k c) -> p k c", k=KD)
        wk = w_in[0].rearrange("(k p) c -> p k c", p=P)
        sp_chunk(sp, SPC, [(r[:, :, 64:96], wk[:, :, C_KR:C_KR + 32]),
                           (r[:, :, 96:112], wk[:, :, C_KR + 16:C_KR + 32]),
                           (r[:, :, 112:128], wk[:, :, C_KR:C_KR + 16]),
                           (r[:, :, 0:8], wk[:, :, C_I:C_I + 8]),
                           (r[:, :, 32:40], wk[:, :, C_F:C_F + 8])])
        for j in range(4):
            cols4(sp, MQK + j, w_in, j % 2, C_MQ + 256 * (j // 2))
        for j in range(2):
            r = raw(UQ + j).rearrange("p (k h c) -> p k h c", k=2, h=4)
            q4 = w["mla_w_uq"][0].rearrange("(k p) (h c) -> p k h c", p=P, c=NOPE + ROPE)
            pcs = []
            s = (UQ + j) % RING
            sp.wait_ge(w_lo_done, UQ + j - RING + 1)
            for dst0, c0, c1 in ((0, 0, 96), (96, 80, 96), (112, 64, 80)):
                for k in range(2):
                    pcs.append((r[:, k, :, dst0:dst0 + c1 - c0], q4[:, k, 4 * j:4 * j + 4, c0:c1]))
            for dst, src in pcs:
                sp.dma_start(dst, src).then_inc(w_loaded[s], 16)
        cols2(sp, UK, w["mla_w_uk"], 0, 0)
        cols2(sp, UV, w["mla_w_uv"], 0, 0)
        for j in range(8):
            cols4(sp, GAC + j, w_in, j % 2, C_G + 256 * (j // 2))
        for j in range(4):
            cols2(sp, MV + j, w_in, 256 * j, C_MV)
        for j in range(4):
            cols2(sp, MO + j, w_in, 256 * j, C_MO)
        for j in range(8):
            cols4(sp, GBC + j, w_in, j % 2, C_G + D + 256 * (j // 2))
        for j in range(4):
            cols4(sp, BA + j, w["w_branch_mla"], 0, 256 * j)
        for j in range(4):
            cols4(sp, BB + j, w["w_branch_ml"], 0, 256 * j)
        for j in range(8):
            cols4(sp, WO + j, w["w_out"], j % 2, 256 * (j // 2))

    MQB = [1, 2, 3, 4]
    QB = [7, 0, 1, 2]
    KVB = [3, 4, 7, 0]
    VB = [1, 2, 3, 4]

    def fm_pair(pe, n, half, banks, a_hi, a_lo, ktiles):
        pe.wait_ge(w_lo_done, n + 1)
        for kk in range(4):
            k = 4 * half + kk
            for f in range(2):
                c = kk * 256 + f * P
                last = three(B[banks[f]][:], wv(n, c, c + P), a_hi[:, k, :], a_lo[:, k, :], k == 0, k == ktiles - 1)
        last.then_inc(w_used, 1)

    def q_padded(hh, c):
        return (mqk if hh % 2 == 0 else tbuf)[:, hh // 2, c * P:(c + 1) * P]

    def mixer_pe(pe):
        lead_pe(pe, 1, CQ)
        pe.wait_ge(w_lo_done, SPC + 1)
        for k in range(KD):
            last = three(B[0][:], wv(SPC, k * P, (k + 1) * P), v_hi[:, k, :], v_lo[:, k, :], k == 0, k == KD - 1)
        last.then_inc(w_used, 1)
        bs[1].wait(pe, "rb_ready", 1)
        fm_pair(pe, MQK, 0, MQB[0:2], v_hi, v_lo, KD)
        pe.wait_ge(ms["cq_sq"], 4)
        for g in range(2):
            for tb in range(TB):
                for f in range(2):
                    last = nc.tensor.matmul(B[5][:, 4 * g + tb:4 * g + tb + 1],
                                            scratch[:, 2 * g + f, tb * P:(tb + 1) * P], ones[:, 0:1],
                                            start=(f == 0), stop=(f == 1))
        last.then_inc(ms["q_sums"], 1)
        fm_pair(pe, MQK + 1, 1, MQB[0:2], v_hi, v_lo, KD)
        fm_pair(pe, MQK + 2, 0, MQB[2:4], v_hi, v_lo, KD)
        pe.wait_ge(ms["rq_ready"], 1)
        bcast_rows(B[6], rq[:, 4:8]).then_inc(ms["rkb_ready"], 1)
        fm_pair(pe, MQK + 3, 1, MQB[2:4], v_hi, v_lo, KD)
        pe.wait_ge(ms["cq_split"], 4)
        for hd in range(HEADS):
            j = UQ + hd // 4
            if hd % 4 == 0:
                pe.wait_ge(w_lo_done, j + 1)
            if hd == 1:
                pe.wait_ge(ms["kr_done"], 1)
            if hd == 2:
                pe.wait_ge(ms["conv_in"], 4)
            if hd >= 4:
                pe.wait_ge(ms["Q_done"], hd - 3)
            for k in range(2):
                c = k * 512 + (hd % 4) * P
                last = three(B[QB[hd % 4]][:], wv(j, c, c + P), cq_hi[:, k, :], cq_lo[:, k, :], k == 0, k == 1)
            if hd % 4 == 3:
                last.then_inc(w_used, 1)
        pe.wait_ge(w_lo_done, UK + 1)
        for pr in range(4):
            if pr == 2:
                pe.wait_ge(ms["Q_done"], 6)
            for k in range(2):
                c = k * 512 + pr * P
                last = three(B[KVB[pr]][:], wv(UK, c, c + P), cq_hi[:, 2 + k, :], cq_lo[:, 2 + k, :], k == 0, k == 1)
        last.then_inc(w_used, 1)
        pe.wait_ge(w_lo_done, UV + 1)
        for tb in range(TB):
            if tb == 0:
                pe.wait_ge(ms["Q_done"], 8)
            if tb == 2:
                pe.wait_ge(ms["K_done"], 4)
            for k in range(2):
                last = three_tm(B[VB[tb]][:], wv(UV, k * 512, (k + 1) * 512), cq_hi[:, 2 + k, tb * P:(tb + 1) * P],
                                cq_lo[:, 2 + k, tb * P:(tb + 1) * P], k == 0, k == 1)
        last.then_inc(w_used, 1)
        pe.wait_ge(ms["Q_done"], HEADS)
        pe.wait_ge(ms["K_done"], HEADS)
        pe.wait_ge(ms["Vm_done"], TB)

        def pv(t):
            hh, b = t // 4, t % 4
            pe.wait_ge(ms["pt_even"] if t % 2 == 0 else ms["pt_odd"], t // 2 + 1)
            if b == 0 and hh >= 1:
                pe.wait_ge(ms["o_done"], hh)
            for kb in range(TB):
                last = nc.tensor.matmul(B[7][:, b * VDIM:(b + 1) * VDIM], PT[:, t % 2, kb * P:(kb + 1) * P],
                                        Vm[:, kb, hh * VDIM:(hh + 1) * VDIM], start=(kb == 0), stop=(kb == TB - 1))
            last.then_inc(ms["pv"], 1)

        for hd in range(HEADS + 1):
            for b in range(TB):
                if hd < HEADS:
                    s = 4 * hd + b
                    if s >= 3:
                        pe.wait_ge(ms["exp"], s - 2)
                    nc.tensor.matmul(B[2 + s % 3][:], Q[:, hd, b * P:(b + 1) * P], K[:, hd, :], start=True,
                                     stop=True).then_inc(ms["scores"], 1)
                if hd >= 1:
                    t = 4 * (hd - 1) + b
                    pe.wait_ge(ms["exp"], t + 1)
                    if t >= 2:
                        pe.wait_ge(ms["pt_even"] if t % 2 == 0 else ms["pt_odd"], t // 2)
                    for kb in range(TB):
                        last = nc.tensor.transpose(B[5 + t % 2][:, kb * P:(kb + 1) * P],
                                                   Pm[:, b, kb * P:(kb + 1) * P], ident[:])
                    last.then_inc(ms["pT"], 1)
                    if t >= 1:
                        pv(t - 1)
            if hd < HEADS:
                if hd % 2 == 0 and hd >= 2:
                    pe.wait_ge(ms["ga"], hd)
                fm_pair(pe, GAC + hd, hd % 2, [0, 1], v_hi, v_lo, KD)
        pv(4 * HEADS - 1)
        MVB, MOB = [2, 3, 4, 7], [0, 1, 5, 6]
        for j in range(4):
            if j == 0:
                pe.wait_ge(ms["o_done"], HEADS)
            if j >= 2:
                pe.wait_ge(ms["oT_split"], j - 1)
            for tb in range(TB):
                last = nc.tensor.transpose(B[5 + j % 2][:, tb * P:(tb + 1) * P], O[:, tb, j * P:(j + 1) * P], ident[:])
            last.then_inc(ms["oTT"], 1)
        def tm_chunk(n0, j, banks):
            pe.wait_ge(w_lo_done, n0 + j + 1)
            for kk in range(2):
                k = 2 * j + kk
                for tb in range(TB):
                    last = three_tm(B[banks[tb]][:], wv(n0 + j, kk * 512, (kk + 1) * 512),
                                    v_hi[:, k, tb * P:(tb + 1) * P], v_lo[:, k, tb * P:(tb + 1) * P],
                                    k == 0, k == KD - 1)
            last.then_inc(w_used, 1)

        for j in range(4):
            tm_chunk(MV, j, MVB)
        pe.wait_ge(ms["ga"], 8)
        pe.wait_ge(ms["oT_split"], 4)
        tm_chunk(MO, 0, MOB)
        tm_chunk(MO, 1, MOB)
        pe.wait_ge(ms["Vml"], TB)
        for d in range(2):
            pe.wait_ge(ms["rows"], d + 1)
            for c in range(TB):
                last = nc.tensor.transpose(B[2 + d][:, c * P:(c + 1) * P], scratch[:, d, c * P:(c + 1) * P], ident[:])
            last.then_inc(ms["RQ_T"], 1)
        pe.wait_ge(ms["mqk_done"], 6)
        for pr in range(2):
            for c in range(TB):
                last = nc.tensor.transpose(B[4 + 3 * pr][:, c * P:(c + 1) * P], mqk[:, 2 + pr, c * P:(c + 1) * P], ident[:])
            last.then_inc(ms["kT_T"], 1)
        tm_chunk(MO, 2, MOB)
        for d in range(2):
            pe.wait_ge(ms["D8"], d + 1)
            if d == 0:
                pe.wait_ge(ms["cx"], 4)
            last = nc.tensor.matmul(B[3][:, 32 * d:32 * d + 32], ones[0:8, :], D8[d][0:8, :], start=True, stop=True)
        last.then_inc(ms["decb_ps"], 1)
        tm_chunk(MO, 3, MOB)
        units = UNITS
        pe.wait_ge(ms["cx"], 4)
        pe.wait_ge(ms["K_tm"], 2)
        pe.wait_ge(ms["decb"], 4)

        def mb(u):
            d, c = units[u]
            if u >= 1:
                pe.wait_ge(ms["Ebig"], 4 * u)
                pe.wait_ge(ms["Sm"], u)
            for hh in range(MLH):
                r = 32 * d + 4 * d + hh
                last = nc.tensor.matmul(B[2][:, hh * P:(hh + 1) * P],
                                        ident[32 * d:32 * d + 8, r:r + 1].broadcast_to([8, P]),
                                        Mrows[32 * d:32 * d + 8, c * P:(c + 1) * P], start=True, stop=True)
            last.then_inc(ms["Mb"], 1)
            for hh in range(MLH):
                last = nc.tensor.matmul(B[7][:, hh * P:(hh + 1) * P], mqk[:, 2 + hh // 2, c * P:(c + 1) * P],
                                        q_padded(hh, c), start=True, stop=True)
            last.then_inc(ms["QK"], 1)

        pe.wait_ge(ms["q_split"], 6)
        mb(0)
        for u in range(8):
            d, c = units[u]
            if u % 2 == 0:
                if u >= 2:
                    pe.wait_ge(ms["gb"], u)
                else:
                    pe.wait_ge(ms["mo"], TB)
            fm_pair(pe, GBC + u, u % 2, [0, 1], v_hi, v_lo, KD)
            if u < 7:
                mb(u + 1)
            first, final = u < 2, u >= 6
            pe.wait_ge(ms["Sm"], u + 1)
            if not final:
                pe.wait_ge(ms["Kp"], u + 1)
            if u >= 1:
                pe.wait_ge(ms["den"], u)
                pe.wait_ge(ms["Cnew"], 6 * min(u, 6))
            for hh in range(MLH):
                nc.tensor.matmul(B[3][:, hh * P:(hh + 1) * P], scratch[:, u % 2, hh * P:(hh + 1) * P],
                                 V[:, c, hh * P:(hh + 1) * P], start=True, stop=True)
                last = nc.tensor.matmul(B[6][:, 64 + hh:65 + hh], scratch[:, u % 2, hh * P:(hh + 1) * P], ones[:, 0:1],
                                        start=True, stop=True)
            if not first:
                for hh in range(MLH):
                    pr, q = hh // 2, q_padded(hh, c)
                    nc.tensor.matmul(B[4][:, hh * P:(hh + 1) * P], q, C[:, d, pr, :], start=True, stop=True)
                    last = nc.tensor.matmul(B[6][:, 68 + hh:69 + hh], q, nstate[:, 2 * d + pr:2 * d + pr + 1],
                                            start=True, stop=True)
            kp = [sqacc[:, 256 * (u % 2) + P * pr:256 * (u % 2) + P * (pr + 1)] for pr in range(2)]
            if not final:
                for pr in range(2):
                    last = nc.tensor.matmul(B[6][:, 72 + pr:73 + pr], kp[pr], ones[:, 0:1], start=True, stop=True)
            last.then_inc(ms["num"], 1)
            if not final:
                for pr in range(2):
                    last = nc.tensor.matmul(B[5][:, 256 * pr:256 * pr + 256], kp[pr], V[:, c, 256 * pr:256 * pr + 256],
                                            start=True, stop=True)
                last.then_inc(ms["Cps"], 1)
        pe.wait_ge(ms["gb"], 8)
        for g in range(4):
            if g == 2:
                pe.wait_ge(ms["den"], 8)
            if g == 3:
                pe.wait_ge(ms["GM"], 2)
            fm_pair(pe, BA + g, 0, BRB[g], oT_hi, oT_lo, 4)
        pe.wait_ge(ms["hn"], 16)
        for j in range(4):
            if j >= 2:
                pe.wait_ge(ms["bT_split"], j - 1)
            for tb in range(TB):
                last = nc.tensor.transpose(B[3 + j % 2][:, tb * P:(tb + 1) * P], HS[:, tb, j * P:(j + 1) * P], ident[:])
            last.then_inc(ms["bTT"], 1)
        pe.wait_ge(ms["bT_split"], 4)
        for g in range(4):
            if g < 3:
                pe.wait_ge(ms["GM"], 2 * g + 4 if g < 2 else 8)
            else:
                pe.wait_ge(ms["b_out"], 2)
            fm_pair(pe, BB + g, 0, BRB[g + 1], bT_hi, bT_lo, 4)
        for g in range(4):
            for half in range(2):
                if g == 0:
                    pe.wait_ge(ms["mixed"], 4 * (half + 1))
                if g == 0 and half == 0:
                    pe.wait_ge(ms["b_out"], 4)
                fm_pair(pe, WO + 2 * g + half, half, [YBANK[2 * g], YBANK[2 * g + 1]], v_hi, v_lo, KD)

    BRB = [(2, 7), (0, 1), (5, 6), (2, 7), (0, 1)]

    UNITS = [(0, 0), (1, 3), (0, 1), (1, 2), (0, 2), (1, 1), (0, 3), (1, 0)]

    def conv_tile(dve, ct):
        o = mqk[:, ct, :]
        wc = VEC["ml_conv_w"]
        for j in range(CONV):
            sc = cols[:, wc + 4 * j + ct:wc + 4 * j + ct + 1]
            src = conv_in[:, ct, j:j + S]
            if j == 0:
                ins = nc.vector.tensor_scalar(o, src, sc, None, ALU.mult)
            else:
                ins = nc.vector.scalar_tensor_tensor(o, src, sc, o, ALU.mult, ALU.add)
            if j < CONV - 1:
                dlink(dve, ins)
            else:
                ins.then_inc(ms["conv_done"], 1)

    def v4(ap):
        return ap.rearrange("p (a b) -> p a b", a=4)

    def mixer_dve(dve):
        lead_dve(dve, 1, CQ)
        dlink(dve, nc.vector.memset(conv_in[:, :, 0:2], 0.0))
        dlink(dve, nc.vector.memset(conv_in[:, :, S + 2:S + 4], 0.0))
        for t in range(4):
            dve_after(dve, CQ + 2 + t // 2)
            nc.vector.tensor_tensor(cq_t[:, t, :], B[4 + t][:], r_b[:], ALU.mult).then_inc(ms["cq_t"], 1)
        for t in range(4):
            dve.wait_ge(ms["cq_t"], t + 1)
            dve.wait_ge(ms["cq_hi"], t + 1)
            g = col("mla_q_norm", t) if t < 2 else col("mla_kv_norm", t - 2)
            nc.vector.scalar_tensor_tensor(cq_lo[:, t, :], cq_t[:, t, :], g, cq_hi[:, t, :].bitcast(F32), ALU.mult,
                                           ALU.subtract).then_inc(ms["cq_split"], 1)
        dve_after(dve, SPC)
        dlink(dve, nc.vector.tensor_tensor(i_row, B[0][0:8, :], r_b[0:8, :], ALU.mult))
        dlink(dve, nc.vector.tensor_scalar(i_row, i_row, ifb[0:8, 0:1], None, ALU.add))
        dlink(dve, nc.vector.tensor_tensor(lf_row, B[0][32:40, :], r_b[32:40, :], ALU.mult))
        dlink(dve, nc.vector.tensor_scalar(lf_row, lf_row, ifb[0:8, 1:2], None, ALU.add))
        dve.wait_ge(ms["q_sums"], 1)
        x = scratch[0:8, 2, :]
        nc.vector.scalar_tensor_tensor(x, lf_row, -1.0, lf_row, ALU.mult, ALU.max).then_inc(ms["f_abs"], 1)
        t0, t1 = scratch[:, 0, :], scratch[:, 1, :]
        dlink(dve, nc.vector.tensor_tensor(t0[64:128, :], B[0][64:128, :], r_b[64:128, :], ALU.mult))
        dlink(dve, nc.vector.tensor_tensor(t0[64:128, :], t0[64:128, :], CS[64:128, :], ALU.mult))
        dlink(dve, nc.vector.tensor_copy(t1[64:96, :], t0[96:128, :]))
        dlink(dve, nc.vector.tensor_tensor(t0[64:96, :], t0[64:96, :], t1[64:96, :], ALU.add))
        rsqrt(dve, rq, B[5][:, 0:8], 8, 1.0 / RANK).then_inc(ms["rq_ready"], 1)
        dlink(dve, nc.vector.tensor_copy(K[64:96, :, :], t0[64:96, None, :].broadcast_to([32, HEADS, S])))
        nc.vector.tensor_copy(K[96:128, :, :], t0[64:96, None, :].broadcast_to([32, HEADS, S])).then_inc(ms["kr_done"], 1)
        dve.wait_ge(ms["rq_ready"], 1)
        dlink(dve, nc.vector.tensor_scalar(rqs, rq[:, 0:4], SCALE, None, ALU.mult))
        dve.wait_ge(ms["f_ln"], 1)
        dlink(dve, nc.vector.scalar_tensor_tensor(lf_row, lf_row, 0.0, x, ALU.min, ALU.subtract))
        for ct in range(4):
            dve_after(dve, MQK + 1 + 2 * (ct // 2))
            nc.vector.tensor_tensor(conv_in[:, ct, 2:S + 2], B[MQB[ct]][:], r_b[:], ALU.mult).then_inc(ms["conv_in"], 1)
        dve.wait_ge(ms["rkb_ready"], 1)
        rkb = scratch[:, 3, :]
        nc.vector.tensor_copy(rkb, B[6][:]).then_inc(ms["rkb_copied"], 1)
        for hd in range(HEADS):
            dve_after(dve, UQ + hd // 4)
            nc.vector.tensor_tensor(Q[:, hd, :], B[QB[hd % 4]][:], CS[:], ALU.mult).then_inc(ms["Q_done"], 1)
        dve.wait_ge(ms["rkb_copied"], 1)
        dve_after(dve, UK)
        for hd in range(HEADS):
            r0 = 64 * (hd % 2)
            nc.vector.tensor_tensor(K[0:64, hd, :], B[KVB[hd // 2]][r0:r0 + 64, :], rkb[r0:r0 + 64, :],
                                    ALU.mult).then_inc(ms["K_done"], 1)
        def o_out(hh):
            dve.wait_ge(ms["exp"], 4 * hh + 4)
            dlink(dve, nc.vector.reciprocal(rsum, sums[:, 4 * hh:4 * hh + 4]))
            dve.wait_ge(ms["pv"], 4 * hh + 4)
            nc.vector.tensor_tensor(O[:, :, hh * VDIM:(hh + 1) * VDIM],
                                    B[7][:, 0:4 * VDIM].rearrange("p (b v) -> p b v", b=4),
                                    rsum[:, :, None].broadcast_to([P, TB, VDIM]), ALU.mult).then_inc(ms["o_done"], 1)
            dve.wait_ge(ms["o_done"], hh + 1)

        def ga_out(g):
            dve_after(dve, GAC + 2 * g + 1)
            for f in range(2):
                nc.vector.tensor_tensor(gates_a[:, 2 * g + f, :], B[f][:], r_b[:], ALU.mult).then_inc(ms["ga"], 1)

        for hd in range(HEADS + 1):
            for b in range(TB):
                if hd < HEADS:
                    s = 4 * hd + b
                    dve.wait_ge(ms["scores"], s + 1)
                    if s >= 4:
                        dve.wait_ge(ms["exp"], s - 3)
                    dlink(dve, nc.vector.tensor_reduce(mx[:, b:b + 1], B[2 + s % 3][:], AX.X, ALU.max))
                    nc.vector.tensor_scalar(nb[:, b:b + 1], mx[:, b:b + 1], rqs[:, b:b + 1], -1.0, ALU.mult,
                                            ALU.mult).then_inc(ms["nb"], 1)
                if hd >= 2 and b == 0:
                    o_out(hd - 2)
                if hd % 2 == 0 and hd >= 2 and b == 1:
                    ga_out(hd // 2 - 1)
                if hd >= 1 and b % 2 == 1:
                    t = 4 * (hd - 1) + b
                    dve.wait_ge(ms["pT"], t + 1)
                    nc.vector.tensor_copy(PT[:, 1, :], B[6][:]).then_inc(ms["pt_odd"], 1)
            if hd < HEADS:
                lo_upto(dve, GAC + hd + 3)
                if hd < 4:
                    conv_tile(dve, hd)
        o_out(HEADS - 1)
        for j in range(4):
            dve.wait_ge(ms["oT_hi"], j + 1)
            nc.vector.tensor_tensor(oT_lo[:, j, :], B[5 + j % 2][:], oT_hi[:, j, :].bitcast(F32),
                                    ALU.subtract).then_inc(ms["oT_split"], 1)
        bb, dd, M = scratch[0:8, 2, :], scratch[0:8, 3, :], sqacc[0:8, :]
        for d in range(2):
            def rv(ap):
                return ap if d == 0 else ap[:, ::-1]
            RQ = scratch[:, d, :]
            dlink(dve, nc.vector.memset(RQ, 0.0))
            dlink(dve, nc.vector.memset(dd, 1.0))
            dlink(dve, nc.vector.memset(dd[:, 0:S:P] if d == 0 else dd[:, P - 1:S:P], 0.0))
            dlink(dve, nc.vector.tensor_tensor_scan(rv(bb), rv(dd), rv(lf_row), 0.0, ALU.mult, ALU.add))
            dlink(dve, nc.vector.tensor_tensor(RQ[0:8, :], i_row, bb, ALU.subtract))
            dlink(dve, nc.vector.memset(dd, 0.0))
            ends = bb[:, P - 1:S - 1:P] if d == 0 else bb[:, P:S:P]
            dlink(dve, nc.vector.tensor_copy(dd[:, P:S:P] if d == 0 else dd[:, P - 1:S - 1:P], ends))
            dlink(dve, nc.vector.tensor_tensor_scan(rv(M), rv(dd), rv(RQ[0:8, :]), 0.0, ALU.add, ALU.max))
            dlink(dve, nc.vector.tensor_copy(Mrows[32 * d:32 * d + 8, :], M))
            dlink(dve, nc.vector.memset(mc[d][0:8, :], 0.0))
            if d == 0:
                dlink(dve, nc.vector.tensor_tensor(mc[d][0:8, 1:4], M[:, P - 1:S - 1:P], bb[:, P - 1:S - 1:P], ALU.add))
                mlast = M[:, P - 1:S:P]
            else:
                dlink(dve, nc.vector.tensor_tensor(mc[d][0:8, 0:3], M[:, P:S:P], bb[:, P:S:P], ALU.add))
                mlast = M[:, 0:S:P]
            lo_upto(dve, MV + 3 + 2 * d)
            nc.vector.tensor_tensor(dcy[d][0:8, :], mc[d][0:8, :], mlast, ALU.subtract).then_inc(ms["dcy"], 1)
            dlink(dve, nc.vector.tensor_tensor(v4(RQ[32:40, :]), mc[d][0:8, :, None].broadcast_to([8, TB, P]), v4(M),
                                               ALU.subtract))
            dlink(dve, nc.vector.scalar_tensor_tensor(RQ[64:72, :], bb, -1.0, M, ALU.mult, ALU.subtract))
            nc.vector.tensor_tensor(v4(RQ[96:104, :]), v4(RQ[0:8, :]),
                                    mlast[:, :, None].broadcast_to([8, TB, P]), ALU.subtract).then_inc(ms["rows"], 1)
            dve.wait_ge(ms["rows"], d + 1)
        lo_upto(dve, MO + 3)
        for d in range(2):
            dve.wait_ge(ms["dexp"], d + 1)
            nc.vector.tensor_tensor(D8[d][0:8, :].rearrange("p (c r) -> p c r", c=4),
                                    ident[0:8, None, 0:8].broadcast_to([8, 4, 8]),
                                    dcy[d][0:8, :, None].broadcast_to([8, 4, 8]), ALU.mult).then_inc(ms["D8"], 1)
        dve.wait_ge(masks_made, 2)
        dve.wait_ge(ms["cx"], 4)
        lo_upto(dve, GBC + 2)

        def ebig(u):
            d, c = UNITS[u]
            dve.wait_ge(ms["Mb"], u + 1)
            if u >= 2:
                dve.wait_ge(ms["num"], u - 1)
            for hh in range(MLH):
                nc.vector.scalar_tensor_tensor(scratch[:, u % 2, hh * P:(hh + 1) * P], B[2][:, hh * P:(hh + 1) * P],
                                               cx[:, d, c, 0, 4 * d + hh:4 * d + hh + 1], maskbig[:, d, :],
                                               ALU.subtract, ALU.max).then_inc(ms["Ebig"], 1)

        def gb_out(g):
            dve_after(dve, GBC + 2 * g + 1)
            for f in range(2):
                nc.vector.tensor_tensor(gates_b[:, 2 * g + f, :], B[f][:], r_b[:], ALU.mult).then_inc(ms["gb"], 1)

        ebig(0)
        for u in range(8):
            d, c = UNITS[u]
            dve.wait_ge(ms["Eexp"], u + 1)
            dve.wait_ge(ms["QK"], u + 1)
            nc.vector.tensor_tensor(scratch[:, u % 2, :], scratch[:, u % 2, :], B[7][:], ALU.mult).then_inc(ms["Sm"], 1)
            lo_upto(dve, GBC + u + 3)
            if u < 7:
                ebig(u + 1)
            if u % 2 == 1:
                gb_out(u // 2)
            dve.wait_ge(ms["num"], u + 1)
            if u >= 2:
                dve.wait_ge(ms["hs"], u - 1)
            tmp, dn4 = scratch[:, 2 + u % 2, :], den[:, 4 * (u % 2):4 * (u % 2) + 4]
            inter = cx[:, d, c, 1, 4 * d:4 * d + 4]
            floor = cx[:, d, c, 2, 4 * d:4 * d + 4]
            if u < 2:
                dlink(dve, nc.vector.tensor_copy(tmp, B[3][:]))
                dlink(dve, nc.vector.tensor_copy(dn4, B[6][:, 64:68]))
            else:
                dlink(dve, nc.vector.tensor_tensor(v4(tmp), v4(B[4][:]), inter[:, :, None].broadcast_to([P, MLH, P]),
                                                   ALU.mult))
                dlink(dve, nc.vector.tensor_tensor(tmp, tmp, B[3][:], ALU.add))
                dlink(dve, nc.vector.tensor_tensor(dn4, B[6][:, 68:72], inter, ALU.mult))
                dlink(dve, nc.vector.tensor_tensor(dn4, dn4, B[6][:, 64:68], ALU.add))
            dlink(dve, nc.vector.scalar_tensor_tensor(dn4, dn4, -1.0, dn4, ALU.mult, ALU.max))
            dlink(dve, nc.vector.tensor_tensor(dn4, dn4, floor, ALU.max))
            nc.vector.reciprocal(dn4, dn4).then_inc(ms["den"], 1)
            if u < 6:
                dve.wait_ge(ms["Cps"], u + 1)
                for hh in range(MLH):
                    b0, pr = 64 * (hh % 2), hh // 2
                    src = B[5][b0:b0 + 64, 256 * pr + P * (hh % 2):256 * pr + P * (hh % 2) + P]
                    st = C[b0:b0 + 64, d, pr, :]
                    if u < 2:
                        nc.vector.tensor_copy(st, src).then_inc(ms["Cnew"], 1)
                    else:
                        dc = decb[b0:b0 + 64, 8 * d + 2 * c + pr:8 * d + 2 * c + pr + 1]
                        nc.vector.scalar_tensor_tensor(st, st, dc, src, ALU.mult, ALU.add).then_inc(ms["Cnew"], 1)
                for pr in range(2):
                    st = nstate[:, 2 * d + pr:2 * d + pr + 1]
                    if u < 2:
                        nc.vector.tensor_copy(st, B[6][:, 72 + pr:73 + pr]).then_inc(ms["Cnew"], 1)
                    else:
                        dc = decb[:, 8 * d + 2 * c + pr:8 * d + 2 * c + pr + 1]
                        nc.vector.scalar_tensor_tensor(st, st, dc, B[6][:, 72 + pr:73 + pr], ALU.mult,
                                                       ALU.add).then_inc(ms["Cnew"], 1)
                dve.wait_ge(ms["Cnew"], 6 * (u + 1))
        def gate_mla(g):
            dve_after(dve, BA + g)
            for f in range(2):
                m = 2 * g + f
                dve.wait_ge(ms["ga_sig"], m + 1)
                nc.vector.tensor_tensor(gates_a[:, m, :], B[BRB[g][f]][:], gates_a[:, m, :], ALU.mult).then_inc(ms["GM"], 1)

        gate_mla(0)
        dve.wait_ge(ms["hn_sq"], 16)
        dve.wait_ge(ms["og"], TB)
        dlink(dve, rsqrt(dve, hrs, hsq, 16, 1.0 / MLV))
        for tb in range(TB):
            for hh in range(MLH):
                o = HS[:, tb, hh * P:(hh + 1) * P]
                last = nc.vector.scalar_tensor_tensor(o, o, hrs[:, 4 * tb + hh:4 * tb + hh + 1],
                                                      og[:, tb, hh * P:(hh + 1) * P], ALU.mult, ALU.mult)
                last.then_inc(ms["hn"], 1)
        for g in range(1, 4):
            gate_mla(g)
        for j in range(4):
            dve.wait_ge(ms["bT_hi"], j + 1)
            nc.vector.scalar_tensor_tensor(bT_lo[:, j, :], B[3 + j % 2][:], col("ml_head_norm", j),
                                           bT_hi[:, j, :].bitcast(F32), ALU.mult, ALU.subtract).then_inc(ms["bT_split"], 1)

        def mix_lo(m):
            dve.wait_ge(ms["mixhi"], m + 1)
            nc.vector.tensor_tensor(v_lo[:, m, :], gates_b[:, m, :], v_hi[:, m, :].bitcast(F32),
                                    ALU.subtract).then_inc(ms["mixed"], 1)
        for g in range(4):
            dve_after(dve, BB + g)
            for f in range(2):
                m = 2 * g + f
                dve.wait_ge(ms["gb_sig"], m + 1)
                nc.vector.tensor_tensor(gates_b[:, m, :], B[BRB[g + 1][f]][:], gates_b[:, m, :], ALU.mult).then_inc(ms["b_out"], 1)
                dve.wait_ge(ms["b_out"], m + 1)
                nc.vector.tensor_tensor(gates_b[:, m, :], gates_a[:, m, :], gates_b[:, m, :],
                                        ALU.add).then_inc(ms["mx_t"], 1)
                dve.wait_ge(ms["mx_t"], m + 1)
                if m >= 1:
                    mix_lo(m - 1)
        mix_lo(7)

    def mixer_act(act):
        lead_act(act, 1, CQ)
        bs[1].wait(act, "h_acc", KD)
        for t in range(4):
            hi_upto(act, CQ + 4 + 2 * (t // 2))
            act.wait_ge(ms["cq_t"], t + 1)
            g = col("mla_q_norm", t) if t < 2 else col("mla_kv_norm", t - 2)
            nc.scalar.activation(cq_hi[:, t, :], cq_t[:, t, :], ACT.Copy, scale=g).then_inc(ms["cq_hi"], 1)
            nc.scalar.activation(scratch[:, t, :], cq_t[:, t, :], ACT.Square).then_inc(ms["cq_sq"], 1)
        hi_upto(act, SPC + 3)
        act.wait_ge(ms["f_abs"], 1)
        x = scratch[0:8, 2, :]
        alink(act, nc.scalar.activation(x, x, ACT.Exp, scale=-1.0))
        nc.scalar.activation(x, x, ACT.Ln, bias=1.0).then_inc(ms["f_ln"], 1)
        act_after(act, UV)
        for tb in range(TB):
            nc.scalar.activation(Vm[:, tb, :], B[VB[tb]][:], ACT.Copy, scale=rq[:, 4 + tb:5 + tb]).then_inc(ms["Vm_done"], 1)
        for hd in range(HEADS + 1):
            for b in range(TB):
                t = 4 * (hd - 1) + b
                if hd >= 1:
                    act.wait_ge(ms["pT"], t + 1)
                if hd < HEADS:
                    s = 4 * hd + b
                    act.wait_ge(ms["nb"], s + 1)
                    nc.scalar.activation(Pm[:, b, :], B[2 + s % 3][:], ACT.Exp, bias=nb[:, b:b + 1],
                                         scale=rqs[:, b:b + 1], accum_out=sums[:, s:s + 1]).then_inc(ms["exp"], 1)
                if hd >= 1 and b % 2 == 0:
                    nc.scalar.activation(PT[:, 0, :], B[5][:], ACT.Copy).then_inc(ms["pt_even"], 1)
            if hd < HEADS:
                hi_upto(act, GAC + hd + 3)
        for j in range(4):
            act.wait_ge(ms["oTT"], j + 1)
            nc.scalar.activation(oT_hi[:, j, :], B[5 + j % 2][:], ACT.Copy).then_inc(ms["oT_hi"], 1)
        for m in range(8):
            act.wait_ge(ms["ga"], m + 1)
            nc.scalar.activation(gates_a[:, m, :], gates_a[:, m, :], ACT.Sigmoid).then_inc(ms["ga_sig"], 1)
        hi_upto(act, MV + 2)
        for ct in range(4):
            act.wait_ge(ms["conv_done"], ct + 1)
            nc.scalar.activation(mqk[:, ct, :], mqk[:, ct, :], ACT.Silu,
                                 bias=col("ml_conv_b", ct)).then_inc(ms["mqk_done"], 1)
        act_after(act, MV + 3)
        for tb in range(TB):
            nc.scalar.activation(V[:, tb, :], B[[2, 3, 4, 7][tb]][:], ACT.Copy, scale=rc[:, tb:tb + 1]).then_inc(ms["Vml"], 1)
        for d in range(2):
            act.wait_ge(ms["dcy"], d + 1)
            nc.scalar.activation(dcy[d][0:8, :], dcy[d][0:8, :], ACT.Exp).then_inc(ms["dexp"], 1)
        hi_upto(act, MO + 3)
        for d in range(2):
            act.wait_ge(ms["RQ_T"], d + 1)
            src = B[2 + d][:].rearrange("p (c q r) -> p c q r", c=4, q=4)
            nc.scalar.activation(cx[:, d, :, 0, :], src[:, :, 0, 0:8], ACT.Copy).then_inc(ms["cx"], 1)
            nc.scalar.activation(cx[:, d, :, 1:4, :], src[:, :, 1:4, 0:8], ACT.Exp).then_inc(ms["cx"], 1)
        for pr in range(2):
            act.wait_ge(ms["kT_T"], pr + 1)
            nc.scalar.activation(K_tm[:, :, pr * P:(pr + 1) * P], v4(B[4 + 3 * pr][:]), ACT.Copy).then_inc(ms["K_tm"], 1)
        act.wait_ge(ms["decb_ps"], 1)
        for d in range(2):
            for par in range(2):
                r = slice(64 * par, 64 * par + 64)
                src = B[3][r, 32 * d:32 * d + 32].rearrange("p (c r) -> p c r", c=4)[:, :, 4 * d + par:4 * d + par + 3:2]
                nc.scalar.activation(decb[r, 8 * d:8 * d + 8].rearrange("p (c r) -> p c r", c=4), src,
                                     ACT.Copy).then_inc(ms["decb"], 1)
        act_after(act, MO + 3)
        for tb in range(TB):
            nc.scalar.activation(og[:, tb, :], B[[0, 1, 5, 6][tb]][:], ACT.Copy,
                                 scale=rc[:, tb:tb + 1]).then_inc(ms["mo"], 1)
        for u in range(8):
            act.wait_ge(ms["Ebig"], 4 * u + 4)
            nc.scalar.activation(scratch[:, u % 2, :], scratch[:, u % 2, :], ACT.Exp, scale=-1.0).then_inc(ms["Eexp"], 1)
            hi_upto(act, GBC + u + 3)
        hi_upto(act, GBC + 10)
        for tb in range(TB):
            act.wait_ge(ms["mo"], TB)
            nc.scalar.activation(og[:, tb, :], og[:, tb, :], ACT.Sigmoid).then_inc(ms["og"], 1)

        def head_squares(i):
            act.wait_ge(ms["hs"], 5 + i)
            tb = HN_ORDER[i]
            if i == 0:
                act.wait_ge(ms["Kp"], 6)
            for hh in range(MLH):
                squares = (K_tm[:, 2 * i + hh // 2, (hh % 2) * P:(hh % 2) * P + P] if i < 2 else
                           (hn_junk[:] if i == 2 else scratch[:, 3, :])[:, hh * P:(hh + 1) * P])
                nc.scalar.activation(squares, HS[:, tb, hh * P:(hh + 1) * P], ACT.Square,
                                     accum_out=hsq[:, 4 * tb + hh:4 * tb + hh + 1]).then_inc(ms["hn_sq"], 1)

        def gb_sigmoid(m):
            act.wait_ge(ms["gb"], m + 1)
            nc.scalar.activation(gates_b[:, m, :], gates_b[:, m, :], ACT.Sigmoid).then_inc(ms["gb_sig"], 1)

        for i in range(3):
            head_squares(i)
        for m in range(4):
            gb_sigmoid(m)
        head_squares(3)
        for m in range(4, 8):
            gb_sigmoid(m)
        hi_upto(act, BA + 6)
        for j in range(4):
            act.wait_ge(ms["bTT"], j + 1)
            nc.scalar.activation(bT_hi[:, j, :], B[3 + j % 2][:], ACT.Copy,
                                 scale=col("ml_head_norm", j)).then_inc(ms["bT_hi"], 1)
        for m in range(8):
            hi_upto(act, BB + 3 + m // 2)
            act.wait_ge(ms["mx_t"], m + 1)
            nc.scalar.activation(v_hi[:, m, :], gates_b[:, m, :], ACT.Copy).then_inc(ms["mixhi"], 1)

    HN_ORDER = [c for _, c in UNITS[4:]]

    def mixer_pool(pool):
        for ct in (2, 3):
            pool.wait_ge(ms["mqk_done"], 4)
            nc.gpsimd.tensor_scalar(mqk[:, ct, :], mqk[:, ct, :], float(MLQK ** -0.5), None, ALU.mult).then_inc(ms["mqk_done"], 1)
        pool.wait_ge(ms["rows"], 2)
        pool.wait_ge(ms["mqk_done"], 6)
        for ct in range(2):
            nc.gpsimd.tensor_copy(tbuf[64:128, ct, :], mqk[64:128, ct, :]).then_inc(ms["q_split"], 1)
            pool.wait_ge(ms["q_split"], 3 * ct + 1)
            nc.gpsimd.memset(tbuf[0:64, ct, :], 0.0).then_inc(ms["q_split"], 1)
            pool.wait_ge(ms["q_split"], 3 * ct + 2)
            nc.gpsimd.memset(mqk[64:128, ct, :], 0.0).then_inc(ms["q_split"], 1)
            pool.wait_ge(ms["q_split"], 3 * ct + 3)
        pool.wait_ge(ms["cx"], 4)
        pool.wait_ge(ms["K_tm"], 2)
        for u in range(9):
            if u < 6:
                d, c = UNITS[u]
                if u >= 2:
                    pool.wait_ge(ms["Cps"], u - 1)
                nc.gpsimd.tensor_tensor(v4(sqacc[:, 256 * (u % 2):256 * (u % 2) + 256]), v4(K_tm[:, c, :]),
                                        cx[:, d, c, 3, 4 * d:4 * d + 4][:, :, None].broadcast_to([P, MLH, MLQK]),
                                        ALU.mult).then_inc(ms["Kp"], 1)
            if u >= 1:
                x = u - 1
                d, c = UNITS[x]
                pool.wait_ge(ms["den"], x + 1)
                tmp = v4(scratch[:, 2 + x % 2, :])
                rd = den[:, 4 * (x % 2):4 * (x % 2) + 4][:, :, None].broadcast_to([P, MLH, P])
                if x < 4:
                    nc.gpsimd.tensor_tensor(v4(HS[:, c, :]), tmp, rd, ALU.mult).then_inc(ms["hs"], 1)
                else:
                    plink(pool, nc.gpsimd.tensor_tensor(tmp, tmp, rd, ALU.mult))
                    pool.wait_ge(ms["hs"], 4)
                    nc.gpsimd.tensor_tensor(HS[:, c, :], HS[:, c, :], scratch[:, 2 + x % 2, :], ALU.add).then_inc(ms["hs"], 1)

    def y_wo(after):
        return lambda eng, p: after(eng, WO + 2 * (p // 2) + 1)

    def y_dn(f):
        return f[4]

    ps = Signals("ple")
    EB = [5, 6, 7, 1]

    def p_embed_pe(pe):
        for k in range(2):
            for tb in range(TB):
                last = nc.tensor.transpose(B[EB[k]][:, tb * P:(tb + 1) * P], p_tm[tb // 2][:, tb % 2, k * P:(k + 1) * P], ident[:])
            last.then_inc(ps["pT"], 1)

    def e_filler(pe):
        def run(i):
            if i == 0:
                pe.wait_ge(p_in, 32)
                p_embed_pe(pe)
                pe.wait_ge(ps["pT_split"], 2)
            if i == 1:
                pe.wait_ge(ps["e_out"], 4)
            pe.wait_ge(w_lo_done, EP + i + 1)
            for q in range(4):
                for k in range(2):
                    c = k * 512 + q * P
                    last = three(B[EB[q]][:], wv(EP + i, c, c + P), pT_hi[:, k, :], pT_lo[:, k, :], k == 0, k == 1)
            last.then_inc(w_used, 1)
        return run

    def pT_act(act):
        for k in range(2):
            act.wait_ge(ps["pT"], k + 1)
            nc.scalar.activation(pT_hi[:, k, :], B[EB[k]][:], ACT.Copy).then_inc(ps["pT_hi"], 1)

    def pT_dve(dve):
        for k in range(2):
            dve.wait_ge(ps["pT_hi"], k + 1)
            nc.vector.tensor_tensor(pT_lo[:, k, :], B[EB[k]][:], pT_hi[:, k, :].bitcast(F32),
                                    ALU.subtract).then_inc(ps["pT_split"], 1)

    def e_act(act, i):
        hi_upto(act, EP + i + 3)
        act.wait_ge(w_used, EP + i + 1)
        for q in range(4):
            nc.scalar.activation(e_sb[:, 4 * i + q, :], B[EB[q]][:], ACT.Copy).then_inc(ps["e_out"], 1)

    def gate_pe(pe):
        pe.wait_ge(ps["e_out"], 8)
        lead_pe(pe, 3, PG)
        bs[3].wait(pe, "rb_ready", 1)
        for g in (2, 3):
            for half in range(2):
                fm_pair(pe, PG + 2 * g + half, half, [2 * (g - 2), 2 * (g - 2) + 1], v_hi, v_lo, KD)


    def gate_dve(dve):
        lead_dve(dve, 3, PG)

        def scale(m):
            dve_after(dve, PG + (2 + m // 2 if m < 4 else 2 * (m // 2) + 1))
            nc.vector.tensor_tensor(ys[:, m, :], B[YBANK[m]][:], r_b[:], ALU.mult).then_inc(ps["g_scaled"], 1)

        def times_e(m):
            dve.wait_ge(ps["g_sig"], m + 1)
            nc.vector.tensor_tensor(ys[:, m, :], ys[:, m, :], e_sb[:, m, :], ALU.mult).then_inc(ps["gy"], 1)
        for m in range(KD):
            scale(m)
            if m >= 1:
                times_e(m - 1)
        times_e(KD - 1)
        dve.wait_ge(ps["gy"], KD)
        post_norm_dve(dve, 4, None)
        for m in range(KD):
            h_tile_dve(dve, 4, m, gain("ple_post_norm"))
            if m >= 2 and m % 2 == 0:
                o_copy_dve(dve, m - 2)
        o_copy_dve(dve, 6)

    OB = [1, 2, 3, 5]

    def o_copy_dve(dve, m):
        dve.wait_ge(ps["o_T"], m + 1)
        nc.vector.tensor_copy(o_sb[:, :, m * P:(m + 1) * P], v4(B[OB[m % 4]][:])).then_inc(ps["o_out"], 1)

    def gate_act(act):
        lead_act(act, 3, PG)
        b = bs[4]
        for m in range(KD):
            hi_upto(act, PG + 4 + 2 * (m // 2))
            act.wait_ge(ps["g_scaled"], m + 1)
            nc.scalar.activation(ys[:, m, :], ys[:, m, :], ACT.Sigmoid).then_inc(ps["g_sig"], 1)
            if m >= 1:
                gsq(act, m - 1)
        gsq(act, KD - 1)
        for m in range(1, KD, 2):
            act.wait_ge(ps["o_T"], m + 1)
            nc.scalar.activation(o_sb[:, :, m * P:(m + 1) * P], v4(B[OB[m % 4]][:]), ACT.Copy).then_inc(o_act, 1)

    o_act = sem("o_act")

    def gsq(act, p):
        b = bs[4]
        act.wait_ge(ps["gy"], p + 1)
        if p >= 4:
            b.wait(act, "y_sum", p - 3)
        else:
            bs[3].wait(act, "h_acc", KD)
        nc.scalar.activation(scratch[:, p % 4, :], ys[:, p, :], ACT.Square).then_inc(b["ysq_act"], 1)

    def final_pe(pe):
        b = bs[4]
        for p in range(KD):
            b.wait(pe, "ysq_act", p + 1)
            for tb in range(TB):
                last = nc.tensor.matmul(B[YBANK[0]][:, tb:tb + 1], scratch[:, p % 4, tb * P:(tb + 1) * P],
                                        ones[:, 0:1], start=(p == 0 and tb == 0), stop=(p == KD - 1),
                                        skip_group_check=True)
            last.then_inc(b["y_sum"], 1)
        b.wait(pe, "r1_ready", 1)
        bcast_rows(B[R1_BANK], r1c).then_inc(b["r1b_ready"], 1)
        for m in range(KD):
            b.wait(pe, "h_ready", m + 1)
            if m >= 4:
                pe.wait_ge(ps["o_out"] if m % 2 == 0 else o_act, (m - 4) // 2 + 1)
            for tb in range(TB):
                last = nc.tensor.transpose(B[OB[m % 4]][:, tb * P:(tb + 1) * P], h[:, m, tb * P:(tb + 1) * P], ident[:])
            last.then_inc(ps["o_T"], 1)

    block = ctx.enter_context(nc.Block())

    @block.sync
    def _(sp):
        sp.dma_start(ident[:], const["ident"]).then_inc(consts_in, 16)
        sp.dma_start(x_tm[:], w["x"][0].rearrange("(b p) d -> p b d", p=P)).then_inc(x_in, 16)
        r = 0
        for name, rows in VEC_ROWS:
            src = w[name][0]
            src = src.rearrange("j (m p) -> (j m) p", p=P) if name == "ml_conv_w" else src.rearrange("(m p) -> m p", p=P)
            sp.dma_start(vec_rows[r:r + rows, :], src).then_inc(consts_in, 16)
            r += rows
        sp.dma_start(ifb[0:8, 0:1], w["ml_i_bias"].rearrange("a d h -> (d h) a")).then_inc(consts_in, 16)
        sp.dma_start(ifb[0:8, 1:2], w["ml_f_bias"].rearrange("a d h -> (d h) a")).then_inc(consts_in, 16)
        sp.dma_start(trig[:], const["trig"]).then_inc(pos_in, 16)
        sp.dma_start(pos_i[:], w["positions"].broadcast_to([P, S])).then_inc(pos_in, 16)
        f1[0](sp)
        mixer_sp(sp)
        f2[0](sp)
        for i in range(2):
            sp.dma_start(p_tm[i][:], w["p"][0, 0, 256 * i:256 * i + 256].rearrange("(b p) d -> p b d", p=P)).then_inc(p_in, 16)
        for j in range(2):
            cols2(sp, EP + j, w["ple_w_proj"], 0, 512 * j)
        for j in range(8):
            half, g = (j // 2, j % 2) if j < 4 else (j % 2, j // 2)
            cols4(sp, PG + j, w["ple_w_gate"], half, 256 * g)
        for q in range(4):
            sp.wait_ge(ps["o_out"], q + 1)
            sp.wait_ge(o_act, q + 1)
            sp.dma_start(out[0, :, q * 256:(q + 1) * 256].rearrange("(b p) d -> p b d", p=P),
                         o_sb[:, :, q * 256:(q + 1) * 256]).then_inc(out_stored, 16)
        sp.wait_ge(out_stored, 64)

    @block.gpsimd
    def _(pool):
        nc.gpsimd.memset(ones[:], 1.0).then_inc(ones_made, 1)
        h_squares_pool(pool, 0)
        h_squares_pool(pool, 1)
        bs[1].wait(pool, "y_sum", KD)
        plink(pool, nc.gpsimd.memset(maskbig[:], 0.0))
        for d in range(2):
            sgn = 1 if d == 0 else -1
            nc.gpsimd.affine_select(out=maskbig[:, d, :], in_=maskbig[:, d, :], compare_op=ALU.is_ge, fill=BIG, base=0,
                                    pattern=[[sgn, P]], channel_multiplier=-sgn).then_inc(masks_made, 1)
        mixer_pool(pool)
        h_squares_pool(pool, 2)
        h_squares_pool(pool, 3)

    @block.vector
    def _(dve):
        dve.wait_ge(vecs_T, 1)
        dlink(dve, nc.vector.tensor_copy(cols[:], B[3][:, 0:NVEC]))
        nc.vector.tensor_scalar(halfpost[:, 0:8], cols[:, VEC["ffn1_post_norm"]:VEC["ffn1_post_norm"] + 8], 0.5, None, ALU.mult)
        nc.vector.tensor_scalar(halfpost[:, 8:16], cols[:, VEC["ffn2_post_norm"]:VEC["ffn2_post_norm"] + 8], 0.5, None, ALU.mult).then_inc(cols_ready, 1)
        b = bs[0]
        for m in range(KD):
            b.wait(dve, "y_ready", m + 1)
            nc.vector.tensor_copy(h[:, m, :], B[YBANK[m]][:]).then_inc(b["h_ready"], 1)
            if m >= 1:
                v_lo_dve(dve, 0, m - 1, gain("ffn1_pre_norm"))
            if m < 3:
                lo_upto(dve, m)
        v_lo_dve(dve, 0, KD - 1, gain("ffn1_pre_norm"))
        dve.wait_ge(pos_in, 32)
        dlink(dve, nc.vector.tensor_copy(turns[:], pos_i[:]))
        dlink(dve, nc.vector.tensor_scalar(ang[:], turns[:], trig[:, 0:1], None, ALU.mult))
        dlink(dve, nc.vector.tensor_scalar(turns[:], ang[:], float(1 / (2 * np.pi)), trig[:, 1:2], ALU.mult, ALU.add))
        magic = float(1.5 * 2 ** 23)
        dlink(dve, nc.vector.tensor_scalar(turns[:], turns[:], magic, None, ALU.add))
        dlink(dve, nc.vector.tensor_scalar(turns[:], turns[:], -magic, None, ALU.add))
        for piece in TWO_PI:
            dlink(dve, nc.vector.scalar_tensor_tensor(ang[:], turns[:], -piece, ang[:], ALU.mult, ALU.add))
        dlink(dve, nc.vector.tensor_scalar(CS[:], ang[:], trig[:, 3:4], None, ALU.add))
        lim = float(np.float32(3.1415925))
        nc.vector.tensor_scalar(CS[:], CS[:], lim, -lim, ALU.min, ALU.max).then_inc(ang_ready, 1)
        dve.wait_ge(cs_ready, 1)
        dlink(dve, nc.vector.memset(CS[0:64, :], 1.0))
        f1[2](dve)
        for p in range(1, KD, 2):
            y_tile(1, True, dve, p, f1[4], ybank)
        boundary_dve(dve, 1, half_post(0), gain("mix_pre_norm"))
        mixer_dve(dve)
        for p in range(1, KD, 2):
            y_tile(2, True, dve, p, y_wo(dve_after), ybank)
        boundary_dve(dve, 2, gain("mix_post_norm"), gain("ffn2_pre_norm"))
        f2[2](dve)
        for p in range(1, KD, 2):
            y_tile(3, True, dve, p, f2[4], ybank)
        bs[3].wait(dve, "y_sum", KD)
        rsqrt(dve, r1c, B[YBANK[0]][:, 0:TB], TB, 1.0 / D).then_inc(bs[3]["r1_ready"], 1)
        pT_dve(dve)
        lo_upto(dve, EP + 2)
        bs[3].wait(dve, "r1b_ready", 1)
        lo_upto(dve, EP + 4)
        for m in range(KD):
            h_tile_dve(dve, 3, m, half_post(1))
            if m >= 1:
                v_lo_dve(dve, 3, m - 1, gain("ple_pre_norm"))
        v_lo_dve(dve, 3, KD - 1, gain("ple_pre_norm"))
        gate_dve(dve)

    @block.scalar
    def _(act):
        act.wait_ge(cols_ready, 1)
        for j in range(3):
            hi_upto(act, j)
        v_tiles_act(act, 0, gain("ffn1_pre_norm"))
        act.wait_ge(ang_ready, 1)
        nc.scalar.activation(CS[:], CS[:], ACT.Sin, scale=trig[:, 2:3]).then_inc(cs_ready, 1)
        f1[3](act)
        for p in range(0, KD, 2):
            y_tile(1, False, act, p, f1[4], ybank)
        v_tiles_act(act, 1, gain("mix_pre_norm"))
        mixer_act(act)
        for p in range(0, KD, 2):
            y_tile(2, False, act, p, y_wo(act_after), ybank)
        hi_upto(act, UP2 + 2)
        v_tiles_act(act, 2, gain("ffn2_pre_norm"))
        f2[3](act)
        for p in range(0, KD, 2):
            y_tile(3, False, act, p, f2[4], ybank)
        pT_act(act)
        e_act(act, 0)
        e_act(act, 1)
        v_tiles_act(act, 3, gain("ple_pre_norm"))
        gate_act(act)

    @block.tensor
    def _(pe):
        pe.wait_ge(consts_in, 16 * (3 + len(VEC_ROWS)))
        pe.wait_ge(ones_made, 1)
        nc.tensor.transpose(B[3][:, 0:NVEC], vec_rows[0:NVEC, :], ident[0:NVEC, 0:NVEC]).then_inc(vecs_T, 1)
        pe.wait_ge(x_in, 16)
        for m in range(KD):
            if m == 7:
                pe.wait_ge(cols_ready, 1)
            for tb in range(TB):
                last = nc.tensor.transpose(B[YBANK[m]][:, tb * P:(tb + 1) * P], x_tm[:, tb, m * P:(m + 1) * P], ident[:])
            last.then_inc(bs[0]["y_ready"], 1)
        f1[1](pe)
        boundary_pe(pe, 1)
        mixer_pe(pe)
        boundary_pe(pe, 2)
        f2[1](pe)
        boundary_pe(pe, 3, e_filler(pe))
        gate_pe(pe)
        final_pe(pe)

    return


TWO_PI = [6.28125, 0.0019350051879882812, 3.019813448190689e-07, 1.0253131677018246e-11]


_OUTS = (1, S, D)


def kernel(**inputs):
    import numpy as _np
    import concourse.bacc as _bacc
    from concourse import mybir as _mybir
    from concourse.bass_utils import run_bass_kernel_spmd as _run

    nc = _bacc.Bacc("TRN2", target_bir_lowering=False, num_devices=1)
    arrays, w = {}, {}
    for name, a in inputs.items():
        a = _np.ascontiguousarray(a)
        arrays[f"in_{name}"] = a
        w[name] = nc.dram_tensor(f"in_{name}", a.shape, _mybir.dt.from_np(a.dtype), kind="ExternalInput").ap()
    ident = _np.eye(P, dtype=_np.float32)
    trig = _np.zeros((P, 4), _np.float32)
    freq = (10000.0 ** (-_np.arange(0, ROPE, 2, dtype=_np.float64) / ROPE)).astype(_np.float32)
    trig[64:128, 0] = _np.tile(freq, 4)
    trig[0:96, 1] = 0.25
    trig[:, 2] = 1.0
    trig[96:112, 2] = -1.0
    trig[0:96, 3] = _np.pi / 2
    arrays["ident"], arrays["trig"] = ident, trig
    const = {k: nc.dram_tensor(k, arrays[k].shape, F32, kind="ExternalInput").ap() for k in ("ident", "trig")}
    out = nc.dram_tensor("out", _OUTS, F32, kind="ExternalOutput").ap()
    program(nc, w, const, out)
    return _run(nc, [arrays], core_ids=[0]).results[0]["out"]
```

```python
from contextlib import ExitStack
import numpy as np
import concourse.bass as bass
from concourse import mybir

ALU = mybir.AluOpType
ACT = mybir.ActivationFunctionType
AX = mybir.AxisListType
F32 = mybir.dt.float32
F32R = mybir.dt.float32r
I32 = mybir.dt.int32

P = 128
S = 512
D = 1024
KD = D // P
TB = S // P
F = 2816
KF = F // P
PLE = 256
EPS = 1e-6
RANK = 256
HEADS, NOPE, ROPE, VDIM = 8, 64, 32, 64
MLH, MLQK, MLV = 4, 64, 128
CONV = 5
BIG = 1e30
SCALE = float((NOPE + ROPE) ** -0.5)
RING = 4
CH = 1024

C_KV, C_KR = RANK, 2 * RANK
C_MQ = C_KR + ROPE
C_MK = C_MQ + MLH * MLQK
C_MV = C_MK + MLH * MLQK
C_I = C_MV + MLH * MLV
C_F = C_I + 2 * MLH
C_MO = C_F + 2 * MLH
C_G = C_MO + MLH * MLV

UP1 = 0
UPN = 4 * (F // 256)
DN1 = UP1 + UPN
CQ = DN1 + KF
SPC = CQ + 4
MQK = SPC + 1
UQ = MQK + 4
UK = UQ + 2
UV = UK + 1
GAC = UV + 1
MV = GAC + 8
MO = MV + 4
GBC = MO + 4
BA = GBC + 8
BB = BA + 4
WO = BB + 4
UP2 = WO + 8
DN2 = UP2 + UPN
EP = DN2 + KF
PG = EP + 2
CHUNKS = PG + 8

VEC_ROWS = [("ffn1_pre_norm", 8), ("ffn1_post_norm", 8), ("mix_pre_norm", 8), ("mix_post_norm", 8),
            ("ffn2_pre_norm", 8), ("ffn2_post_norm", 8), ("ple_pre_norm", 8), ("ple_post_norm", 8),
            ("mla_q_norm", 2), ("mla_kv_norm", 2), ("ml_conv_b", 4), ("ml_conv_w", 4 * CONV),
            ("ml_head_norm", 4)]
VEC = {}
NVEC = 0
for _name, _rows in VEC_ROWS:
    VEC[_name] = NVEC
    NVEC += _rows

YBANK = [4, 5, 6, 7, 0, 1, 2, 3]
ADDED = 6
R1_BANK, HSTAT_BANK, R2_BANK = 0, 2, 3


def loaded_totals():
    dmas = {SPC: 5, UQ: 6, UQ + 1: 6}
    slot, out = [0] * RING, []
    for n in range(CHUNKS):
        slot[n % RING] += 16 * dmas.get(n, 1)
        out.append(slot[n % RING])
    return out


LOADED = loaded_totals()


def program(nc, w, const, out):
    ctx = ExitStack()
    with ctx:
        block_build(nc, w, const, out, ctx)


def block_build(nc, w, const, out, ctx):
    cursor = [(nc.sbuf_base + 63) // 64 * 64]

    def at(name, shape, dt, offset):
        return nc.alloc_sbuf_tensor_at(name, shape, dt, offset=offset)

    def sb(name, shape, dt=F32):
        n = int(np.prod(shape[1:])) * 4
        t = at(name, shape, dt, cursor[0])
        cursor[0] += (n + 31) // 32 * 32
        return t

    h = sb("h", [P, KD, S])
    v_hi = sb("v_hi", [P, KD, S], F32R)
    v_lo = sb("v_lo", [P, KD, S], F32R)
    w_raw = sb("w_raw", [P, RING, CH])
    w_hi = sb("w_hi", [P, RING, CH], F32R)
    w_lo = sb("w_lo", [P, RING, CH], F32R)
    ident = sb("ident", [P, P])
    ones = sb("ones", [P, P])
    cols = sb("cols", [P, NVEC])
    r_b = sb("r_b", [P, S])
    sqacc = sb("sqacc", [P, S])
    scratch = sb("scratch", [P, 4, S])
    small = sb("small", [P, 320])
    A0 = cursor[0]
    KB = 1024
    assert A0 + 97 * KB <= nc.sbuf_usable_end, (A0, nc.sbuf_usable_end)

    def ar(name, shape, kb, dt=F32):
        return at(name, shape, dt, A0 + int(kb * KB))

    prod_hi = ar("prod_hi", [P, KF, S], 0, F32R)
    prod_lo = ar("prod_lo", [P, KF, S], 44, F32R)
    ys = ar("ys", [P, KD, S], 0)
    tbuf = ar("tbuf", [P, 2, S], 90)
    x_tm = ar("x_tm", [P, TB, D], 0)
    vec_rows = ar("vec_rows", [P, P], 20)
    pos_i = ar("pos_i", [P, S], 24, I32)
    ang = ar("ang", [P, S], 26)
    turns = ar("turns", [P, S], 28)
    trig = ar("trig", [P, 4], 96.5)
    CS = ar("CS", [P, S], 88)
    gates_a = ar("gates_a", [P, 8, S], 0)
    cq_t = ar("cq_t", [P, 4, S], 0)
    conv_in = ar("conv_in", [P, 4, S + 4], 8)
    Q = ar("Q", [P, HEADS, S], 16.5)
    K = ar("K", [P, HEADS, S], 32.5)
    Vm = ar("Vm", [P, TB, S], 48.5)
    cq_hi = ar("cq_hi", [P, 4, S], 56.5, F32R)
    cq_lo = ar("cq_lo", [P, 4, S], 64.5, F32R)
    Pm = ar("Pm", [P, TB, S], 56.5)
    O = ar("O", [P, TB, S], 64.5)
    PT = ar("PT", [P, 2, S], 72.5)
    mqk = ar("mqk", [P, 4, S], 76.5)
    lf_row = tbuf[0:8, 0, :]
    i_row = tbuf[0:8, 1, :]
    oT_hi = ar("oT_hi", [P, 4, S], 16.5, F32R)
    oT_lo = ar("oT_lo", [P, 4, S], 24.5, F32R)
    gates_b = ar("gates_b", [P, 8, S], 32.5)
    V = ar("V", [P, TB, S], 48.5)
    og = ar("og", [P, TB, S], 56.5)
    HS = ar("HS", [P, TB, S], 64.5)
    K_tm = ar("K_tm", [P, TB, 256], 72.5)
    C = ar("C", [P, 2, 2, P], 84.5)
    maskbig = ar("maskbig", [P, 2, P], 86.5)
    Mrows = ar("Mrows", [P, S], 88)
    hn_junk = ar("hn_junk", [P, S], 94)
    bT_hi = ar("bT_hi", [P, 4, S], 48.5, F32R)
    bT_lo = ar("bT_lo", [P, 4, S], 76.5, F32R)
    cx = ar("cx", [P, 2, TB, 4, 8], 96)
    e_sb = ar("e_sb", [P, KD, S], 20)
    p_tm = [ar("p_tm0", [P, 2, PLE], 88), ar("p_tm1", [P, 2, PLE], 94)]
    pT_hi = ar("pT_hi", [P, 2, S], 40, F32R)
    pT_lo = ar("pT_lo", [P, 2, S], 44, F32R)
    o_sb = ar("o_sb", [P, TB, D], 50)
    yg = ar("yg", [P, KD, S], 66)

    B = [ctx.enter_context(nc.psum_tensor(f"bank{i}", [P, S], F32)) for i in range(8)]

    used = [0]

    def scol(n):
        a = used[0]
        used[0] += n
        assert used[0] <= 320
        return small[:, a:a + n]

    nw = [scol(16) for _ in range(4)]
    r1c = scol(4)
    rc = scol(4)
    rq = scol(8)
    rqs = scol(4)
    mx = scol(4)
    nb = scol(4)
    sums = scol(32)
    rsum = scol(4)
    halfpost = scol(16)
    nstate = scol(4)
    decb = scol(16)
    den = scol(8)
    hsq = scol(16)
    hrs = scol(16)
    ifb = scol(2)
    mc = [scol(4), scol(4)]
    dcy = [scol(4), scol(4)]
    D8 = [scol(32), scol(32)]

    def sem(name):
        return ctx.enter_context(nc.semaphore(name))

    w_loaded = [sem(f"w_loaded{s}") for s in range(RING)]
    w_hi_done, w_lo_done, w_used = sem("w_hi_done"), sem("w_lo_done"), sem("w_used")
    consts_in, x_in, p_in, pos_in, ident_in, x_late, bias_in = sem("consts_in"), sem("x_in"), sem("p_in"), sem("pos_in"), sem("ident_in"), sem("x_late"), sem("bias_in")
    masks_made = sem("masks_made")
    pool_step, dve_step, act_step = sem("pool_step"), sem("dve_step"), sem("act_step")
    ones_made, vecs_T, cols_ready = sem("ones_made"), sem("vecs_T"), sem("cols_ready")
    ang_ready, cs_ready = sem("ang_ready"), sem("cs_ready")
    out_stored = sem("out_stored")

    class Signals(dict):
        def __init__(self, prefix):
            super().__init__()
            self.prefix = prefix

        def __missing__(self, name):
            self[name] = sem(f"{self.prefix}_{name}")
            return self[name]

    class Boundary:
        signals = Signals("boundary")
        PER = {"y_ready": (8, 7, 0, 7, 0), "ysq_dve": (0, 4, 4, 4, 0), "ysq_act": (0, 4, 4, 4, 8),
               "y_acc": (0, ADDED, ADDED, ADDED, ADDED), "y_sum": (0, 1, 1, 1, 1), "r1_ready": (0, 1, 1, 1, 1), "r1b_ready": (0, 1, 1, 1, 1),
               "h_ready": (8,) * 5, "vhi_ready": (8,) * 5, "v_ready": (8,) * 5, "hsq_ready": (8,) * 5,
               "h_acc": (8,) * 5, "h2_ready": (1,) * 5, "r2_ready": (1,) * 5, "r2b_ready": (1,) * 5,
               "rb_ready": (1,) * 5}

        def __init__(self, n):
            self.n = n

        def __getitem__(self, name):
            return self.signals[name]

        def wait(self, eng, name, value):
            eng.wait_ge(self.signals[name], sum(self.PER[name][:self.n]) + value)

    bs = [Boundary(n) for n in range(5)]

    def three(o, ws, a_hi, a_lo, start, stop):
        whi, wlo = ws
        nc.tensor.matmul(o, whi, a_hi, start=start, stop=False)
        nc.tensor.matmul(o, whi, a_lo, start=False, stop=False)
        return nc.tensor.matmul(o, wlo, a_hi, start=False, stop=stop)

    def three_tm(o, ws, a_hi, a_lo, start, stop):
        whi, wlo = ws
        nc.tensor.matmul(o, a_hi, whi, start=start, stop=False)
        nc.tensor.matmul(o, a_hi, wlo, start=False, stop=False)
        return nc.tensor.matmul(o, a_lo, whi, start=False, stop=stop)

    def wv(n, a, b):
        s = n % RING
        return w_hi[:, s, a:b], w_lo[:, s, a:b]

    def split_hi(act, n, it=0):
        if n >= CHUNKS:
            return
        s = n % RING
        act.wait_ge(w_loaded[s], LOADED[n] + 16 * it)
        if n >= RING or not isinstance(it, int):
            act.wait_ge(w_used, n - RING + 1 + 4 * it)
        nc.scalar.activation(w_hi[:, s, :], w_raw[:, s, :], ACT.Copy).then_inc(w_hi_done, 1)

    def split_lo(dve, n, it=0):
        if n >= CHUNKS:
            return
        s = n % RING
        dve.wait_ge(w_hi_done, n + 1 + 4 * it)
        nc.vector.tensor_tensor(w_lo[:, s, :], w_raw[:, s, :], w_hi[:, s, :].bitcast(F32),
                                ALU.subtract).then_inc(w_lo_done, 1)

    hi_next, lo_next = [0], [0]

    def hi_upto(act, n):
        while hi_next[0] <= min(n, CHUNKS - 1):
            split_hi(act, hi_next[0])
            hi_next[0] += 1

    def lo_upto(dve, n):
        while lo_next[0] <= min(n, CHUNKS - 1):
            split_lo(dve, lo_next[0])
            lo_next[0] += 1

    def act_after(act, n):
        hi_upto(act, n + 3)
        act.wait_ge(w_used, n + 1)

    def dve_after(dve, n):
        lo_upto(dve, n + 3)
        dve.wait_ge(w_used, n + 1)

    dn, an, pn = [0], [0], [0]

    def dlink(dve, ins):
        dn[0] += 1
        ins.then_inc(dve_step, 1)
        dve.wait_ge(dve_step, dn[0])

    def alink(act, ins):
        an[0] += 1
        ins.then_inc(act_step, 1)
        act.wait_ge(act_step, an[0])

    def plink(pool, ins):
        pn[0] += 1
        ins.then_inc(pool_step, 1)
        pool.wait_ge(pool_step, pn[0])

    def rsqrt(dve, dst, src, n, inv):
        x, y, t, u = (a[:, 0:n] for a in nw)
        dlink(dve, nc.vector.tensor_scalar(x, src, inv, EPS, ALU.mult, ALU.add))
        dlink(dve, nc.vector.tensor_scalar(t.bitcast(I32), x.bitcast(I32), 1, None, ALU.logical_shift_right))
        dlink(dve, nc.vector.tensor_scalar(y.bitcast(I32), t.bitcast(I32), -1.0, float(0x5F3759DF),
                                           ALU.mult, ALU.add))
        for k in range(3):
            dlink(dve, nc.vector.scalar_tensor_tensor(t, y, -0.5, y, ALU.mult, ALU.mult))
            dlink(dve, nc.vector.tensor_tensor(u, t, x, ALU.mult))
            last = nc.vector.scalar_tensor_tensor(dst if k == 2 else y, u, 1.5, y, ALU.add, ALU.mult)
            if k < 2:
                dlink(dve, last)
        return last

    def col(name, m):
        c = VEC[name] + m
        return cols[:, c:c + 1]

    def bcast_rows(o, c):
        for tb in range(TB):
            last = nc.tensor.matmul(o[:, tb * P:(tb + 1) * P], c[:, tb:tb + 1].broadcast_to([P, P]), ident[:],
                                    start=True, stop=True)
        return last

    def token_sums(o, src):
        for tb in range(TB):
            last = nc.tensor.matmul(o[:, tb:tb + 1], src[:, tb * P:(tb + 1) * P], ones[:, 0:1], start=True, stop=True)
        return last

    def y_squares_pool(pool, n, p):
        b = bs[n]
        b.wait(pool, "ysq_act" if p % 2 == 0 or n == 4 else "ysq_dve", p + 1 if n == 4 else p // 2 + 1)
        if p == 0:
            nc.gpsimd.tensor_copy(sqacc[:], scratch[:, 0, :]).then_inc(b["y_acc"], 1)
        else:
            b.wait(pool, "y_acc", p)
            nc.gpsimd.tensor_tensor(sqacc[:], sqacc[:], scratch[:, p % 4, :], ALU.add).then_inc(b["y_acc"], 1)

    def y_sums_pe(pe, n, bank):
        b = bs[n]
        for p in range(ADDED - 1, KD):
            if p == ADDED - 1:
                b.wait(pe, "y_acc", ADDED)
            elif n == 4:
                b.wait(pe, "ysq_act", p + 1)
            else:
                b.wait(pe, "ysq_act" if p % 2 == 0 else "ysq_dve", p // 2 + 1)
            src = sqacc[:] if p == ADDED - 1 else scratch[:, p % 4, :]
            for tb in range(TB):
                last = nc.tensor.matmul(B[bank][:, tb:tb + 1], src[:, tb * P:(tb + 1) * P], ones[:, 0:1],
                                        start=(p == ADDED - 1 and tb == 0), stop=(p == KD - 1), skip_group_check=True)
        last.then_inc(b["y_sum"], 1)

    def boundary_pe(pe, n):
        b = bs[n]
        if n == 3:
            p_transposes_pe(pe)
        y_sums_pe(pe, n, YBANK[0])
        if n == 3:
            e_product_pe(pe, 0)
        b.wait(pe, "r1_ready", 1)
        bcast_rows(B[R1_BANK], r1c).then_inc(b["r1b_ready"], 1)
        if n == 3:
            e_product_pe(pe, 1)

    def y_tile(n, dve_side, eng, p, ready, src):
        b = bs[n]
        ready(eng, p)
        if p >= 4:
            b.wait(eng, "y_acc", p - 3)
        if dve_side:
            dlink(eng, nc.vector.tensor_copy(ys[:, p, :], src(p)))
            nc.vector.tensor_tensor(scratch[:, p % 4, :], ys[:, p, :], ys[:, p, :], ALU.mult).then_inc(b["ysq_dve"], 1)
        else:
            alink(eng, nc.scalar.activation(ys[:, p, :], src(p), ACT.Copy))
            nc.scalar.activation(scratch[:, p % 4, :], ys[:, p, :], ACT.Square).then_inc(b["ysq_act"], 1)

    def post_norm_dve(dve, n):
        b = bs[n]
        b.wait(dve, "y_sum", 1)
        rsqrt(dve, r1c, B[YBANK[0]][:, 0:TB], TB, 1.0 / D).then_inc(b["r1_ready"], 1)
        b.wait(dve, "r1b_ready", 1)

    def h_tile_dve(dve, n, m, post):
        b = bs[n]
        t = tbuf[:, m % 2, :]
        dlink(dve, nc.vector.scalar_tensor_tensor(t, ys[:, m, :], post(m), B[R1_BANK][:], ALU.mult, ALU.mult))
        nc.vector.tensor_tensor(h[:, m, :], h[:, m, :], t, ALU.add).then_inc(b["h_ready"], 1)

    def v_lo_dve(dve, n, m, pre):
        b = bs[n]
        b.wait(dve, "vhi_ready", m + 1)
        b.wait(dve, "h_ready", m + 1)
        nc.vector.scalar_tensor_tensor(v_lo[:, m, :], h[:, m, :], pre(m), v_hi[:, m, :].bitcast(F32),
                                       ALU.mult, ALU.subtract).then_inc(b["v_ready"], 1)

    def boundary_dve(dve, n, post, pre):
        post_norm_dve(dve, n)
        for m in range(KD):
            h_tile_dve(dve, n, m, post)
            if m >= 1:
                v_lo_dve(dve, n, m - 1, pre)
        v_lo_dve(dve, n, KD - 1, pre)

    def v_tiles_act(act, n, pre, before={}):
        b = bs[n]
        for m in range(KD):
            if m in before:
                before[m]()
            b.wait(act, "h_ready", m + 1)
            nc.scalar.activation(v_hi[:, m, :], h[:, m, :], ACT.Copy, scale=pre(m)).then_inc(b["vhi_ready"], 1)
            if m >= 4:
                b.wait(act, "h_acc", m - 3)
            nc.scalar.activation(scratch[:, m % 4, :], h[:, m, :], ACT.Square).then_inc(b["hsq_ready"], 1)

    def h_squares_pool(pool, n):
        b = bs[n]
        for m in range(KD):
            b.wait(pool, "hsq_ready", m + 1)
            if m == 0:
                nc.gpsimd.tensor_copy(sqacc[:], scratch[:, 0, :]).then_inc(b["h_acc"], 1)
            else:
                b.wait(pool, "h_acc", m)
                nc.gpsimd.tensor_tensor(sqacc[:], sqacc[:], scratch[:, m % 4, :], ALU.add).then_inc(b["h_acc"], 1)

    def lead_pe(pe, n, N):
        b = bs[n]
        for j in range(4):
            pe.wait_ge(w_lo_done, N + j + 1)
            if n == 3 and j == 1:
                pe.wait_ge(ps["e_out"], 8)
            for kk in range(4):
                k = 4 * (j // 2) + kk
                if j % 2 == 0:
                    b.wait(pe, "vhi_ready", max(k + 1, 2) if n == 0 else k + 1)
                    for f in range(2):
                        c = kk * 256 + f * P
                        o, (whi, wlo) = B[4 + f], wv(N + j, c, c + P)
                        nc.tensor.matmul(o[:], whi, v_hi[:, k, :], start=(k == 0), stop=False)
                        nc.tensor.matmul(o[:], wlo, v_hi[:, k, :], start=False, stop=False)
                    b.wait(pe, "v_ready", k + 1)
                    for f in range(2):
                        c = kk * 256 + f * P
                        last = nc.tensor.matmul(B[4 + f][:], wv(N + j, c, c + P)[0], v_lo[:, k, :], start=False,
                                                stop=(k == KD - 1))
                    continue
                for f in range(2):
                    c = kk * 256 + f * P
                    last = three(B[4 + 2 * (j % 2) + f][:], wv(N + j, c, c + P), v_hi[:, k, :], v_lo[:, k, :],
                                 k == 0, k == KD - 1)
            last.then_inc(w_used, 1)
            if j == 2:
                b.wait(pe, "h_acc", KD)
                token_sums(B[HSTAT_BANK], sqacc).then_inc(b["h2_ready"], 1)
        b.wait(pe, "r2_ready", 1)
        bcast_rows(B[R2_BANK], rc).then_inc(b["r2b_ready"], 1)

    def lead_dve(dve, n, N):
        b = bs[n]
        lo_upto(dve, N + 4)
        b.wait(dve, "h2_ready", 1)
        rsqrt(dve, rc, B[HSTAT_BANK][:, 0:TB], TB, 1.0 / D).then_inc(b["r2_ready"], 1)
        lo_upto(dve, N + 5)
        b.wait(dve, "r2b_ready", 1)
        nc.vector.tensor_copy(r_b[:], B[R2_BANK][:]).then_inc(b["rb_ready"], 1)
        b.wait(dve, "rb_ready", 1)

    def lead_act(act, n, N):
        hi_upto(act, N + 5)

    def ffn(n, N, DN, wg, wu, wd):
        gate0, silu0 = sem(f"f{n}_gate0"), sem(f"f{n}_silu0")
        gate_scaled, silu_done = sem(f"f{n}_gate_scaled"), sem(f"f{n}_silu_done")
        silu_r, prod_done = sem(f"f{n}_silu_r"), sem(f"f{n}_prod_done")
        phi, prod_ready = sem(f"f{n}_phi"), sem(f"f{n}_prod_ready")
        NI = F // 256
        yb = bs[n + 1]

        def sp_load(sp, i, j):
            m = N + j
            up, half = (j // 2, j % 2) if not isinstance(i, int) else (j % 2, j // 2)
            src = (wu if up else wg)[0, half * 512:half * 512 + 512, bass.ds(i * 256, 256)]
            sp.dma_start(w_raw[:, m % RING, :].rearrange("p (k c) -> p k c", k=4),
                         src.rearrange("(k p) c -> p k c", p=P)).then_inc(w_loaded[m % RING], 16)

        def sp_prog(sp):
            for j in range(4):
                if N + j >= RING:
                    sp.wait_ge(w_lo_done, N + j - RING + 1)
                sp_load(sp, 0, j)
            with sp.Fori(1, NI) as i:
                for j in range(4):
                    sp.wait_ge(w_lo_done, 4 * i + (N + j - RING + 1))
                    sp_load(sp, i, j)
            def down(k, j):
                m = DN + j
                sp.wait_ge(w_lo_done, k + (DN - RING + 1))
                sp.dma_start(w_raw[:, m % RING, :], wd[0, bass.ds(k * P, P), :]).then_inc(w_loaded[m % RING], 16)
            with sp.Fori(0, KF // 4) as i:
                for j in range(4):
                    down(4 * i + j, j)
            for j in range(KF // 4 * 4, KF):
                down(j, j)

        def pe_prog(pe):
            lead_pe(pe, n, N)
            with pe.Fori(1, NI) as i:
                for j in range(4):
                    pe.wait_ge(w_lo_done, 4 * i + (N + j + 1))
                    if j == 0:
                        pe.wait_ge(gate_scaled, 2 * i)
                    if j == 2:
                        pe.wait_ge(prod_done, 2 * i)
                    for kk in range(4):
                        k = 4 * (j % 2) + kk
                        for f in range(2):
                            c = kk * 256 + f * P
                            last = three(B[2 * (j // 2) + f][:], wv(N + j, c, c + P), v_hi[:, k, :], v_lo[:, k, :],
                                         k == 0, k == KD - 1)
                    last.then_inc(w_used, 1)

            def down(k, j, first=False):
                pe.wait_ge(w_lo_done, k + (DN + 1))
                ph = prod_hi[:, k, :] if isinstance(k, int) else prod_hi[:, bass.ds(k, 1), :].rearrange("p a s -> p (a s)")
                pl = prod_lo[:, k, :] if isinstance(k, int) else prod_lo[:, bass.ds(k, 1), :].rearrange("p a s -> p (a s)")
                for m in range(KD):
                    if first and m == 4:
                        pe.wait_ge(gate_scaled, 2 * NI)
                    if first and m == 6:
                        pe.wait_ge(prod_done, 2 * NI)
                    last = three(B[YBANK[m]][:], wv(DN + j, m * P, (m + 1) * P), ph, pl, first, False)
                last.then_inc(w_used, 1)

            pe.wait_ge(prod_ready, 2 * (NI - 1))
            for k in range(4):
                down(k, k, first=(k == 0))
            with pe.Fori(1, KF // 4) as i:
                for j in range(4):
                    down(4 * i + j, j)
            pe.wait_ge(prod_ready, 2 * NI)
            tail = range(KF // 4 * 4, KF)
            pe.wait_ge(w_lo_done, DN + KF)
            for m in range(KD):
                for k in tail:
                    last = three(B[YBANK[m]][:], wv(DN + k, m * P, (m + 1) * P), prod_hi[:, k, :], prod_lo[:, k, :],
                                 False, k == KF - 1)
                    if m == KD - 1:
                        last.then_inc(w_used, 1)
                if m < KD - 1:
                    last.then_inc(yb["y_ready"], 1)

        def gates_dve(dve, i, first):
            for f in range(2):
                dve.wait_ge(w_used, 4 * i + (N + (3 if first else 2)))
                if not first:
                    dve.wait_ge(prod_ready, 2 * i + f - 1)
                nc.vector.tensor_tensor(scratch[:, f, :], B[(4 if first else 0) + f][:], r_b[:],
                                        ALU.mult).then_inc(gate0 if first else gate_scaled, 1)
            for f in range(2):
                dve.wait_ge(silu0 if first else silu_done, (f + 1) if first else 2 * i + (f - 1))
                nc.vector.tensor_tensor(scratch[:, f, :], scratch[:, f, :], r_b[:], ALU.mult).then_inc(silu_r, 1)

        def ups_dve(dve, i, first):
            dve.wait_ge(w_used, 4 * i + (N + 4))
            for f in range(2):
                dve.wait_ge(silu_r, 2 * i + (f + 1))
                if not first:
                    dve.wait_ge(phi, 2 * i + (f - 1))
                nc.vector.tensor_tensor(scratch[:, 2 + f, :], B[(6 if first else 2) + f][:], scratch[:, f, :],
                                        ALU.mult).then_inc(prod_done, 1)
            for f in range(2):
                dve.wait_ge(phi, 2 * i + (f + 1))
                o = prod_lo[:, 2 * i + f, :] if first else prod_lo[:, bass.ds(2 * i + f, 1), :].rearrange("p a s -> p (a s)")
                hh = prod_hi[:, 2 * i + f, :] if first else prod_hi[:, bass.ds(2 * i + f, 1), :].rearrange("p a s -> p (a s)")
                nc.vector.tensor_tensor(o, scratch[:, 2 + f, :], hh.bitcast(F32), ALU.subtract).then_inc(prod_ready, 1)

        def dve_prog(dve):
            dve.sem_inc(gate_scaled, 2)
            lead_dve(dve, n, N)
            gates_dve(dve, 0, True)
            lo_upto(dve, N + 6)
            ups_dve(dve, 0, True)
            assert lo_next[0] == N + 7
            with dve.Fori(1, NI) as i:
                for j in range(3):
                    split_lo(dve, N + 3 + j, i)
                gates_dve(dve, i, False)
                split_lo(dve, N + 6, i)
                ups_dve(dve, i, False)
            with dve.Fori(0, KF // 4) as i:
                for j in range(4):
                    split_lo(dve, DN + 3 + j, i)
            lo_next[0] = DN + 3 + KF // 4 * 4
            lo_upto(dve, DN + KF + 1)

        def silu_act(act, i, first):
            for f in range(2):
                act.wait_ge(gate0 if first else gate_scaled, (f + 1) if first else 2 * i + (f + 1))
                nc.scalar.activation(scratch[:, f, :], scratch[:, f, :], ACT.Silu).then_inc(silu0 if first else silu_done, 1)

        def phi_act(act, i, first):
            for f in range(2):
                act.wait_ge(prod_done, 2 * i + (f + 1))
                o = prod_hi[:, 2 * i + f, :] if first else prod_hi[:, bass.ds(2 * i + f, 1), :].rearrange("p a s -> p (a s)")
                nc.scalar.activation(o, scratch[:, 2 + f, :], ACT.Copy).then_inc(phi, 1)

        def act_prog(act):
            lead_act(act, n, N)
            silu_act(act, 0, True)
            hi_upto(act, N + 6)
            phi_act(act, 0, True)
            with act.Fori(1, NI) as i:
                for j in range(3):
                    split_hi(act, N + 3 + j, i)
                silu_act(act, i, False)
                split_hi(act, N + 6, i)
                phi_act(act, i, False)
            with act.Fori(0, KF // 4) as i:
                for j in range(4):
                    split_hi(act, DN + 3 + j, i)
            hi_next[0] = DN + 3 + KF // 4 * 4
            hi_upto(act, DN + KF + 1)

        def y_wait(eng, p):
            if p < KD - 1:
                yb.wait(eng, "y_ready", p + 1)
            else:
                eng.wait_ge(w_used, DN + KF)

        return sp_prog, pe_prog, dve_prog, act_prog, y_wait

    f1 = ffn(0, UP1, DN1, w["ffn1_w_gate"], w["ffn1_w_up"], w["ffn1_w_down"])
    f2 = ffn(2, UP2, DN2, w["ffn2_w_gate"], w["ffn2_w_up"], w["ffn2_w_down"])

    def half_post(a):
        return lambda m: halfpost[:, 8 * a + m:8 * a + m + 1]

    def gain(name):
        return lambda m: col(name, m)

    def ybank(p):
        return B[YBANK[p]][:]

    ms = Signals("mix")

    w_in = w["w_in"]

    def sp_chunk(sp, n, pieces):
        if n >= RING:
            sp.wait_ge(w_lo_done, n - RING + 1)
        for dst, src in pieces:
            sp.dma_start(dst, src).then_inc(w_loaded[n % RING], 16)

    def raw(n):
        return w_raw[:, n % RING, :]

    def cols4(sp, n, wt, half, c0):
        sp_chunk(sp, n, [(raw(n).rearrange("p (k c) -> p k c", k=4),
                          wt[0, half * 512:half * 512 + 512, c0:c0 + 256].rearrange("(k p) c -> p k c", p=P))])

    def cols2(sp, n, wt, r0, c0):
        sp_chunk(sp, n, [(raw(n).rearrange("p (k c) -> p k c", k=2),
                          wt[0, r0:r0 + 256, c0:c0 + 512].rearrange("(k p) c -> p k c", p=P))])

    def mixer_sp(sp):
        for j in range(4):
            cols4(sp, CQ + j, w_in, j // 2, 256 * (j % 2))
        r = raw(SPC).rearrange("p (k c) -> p k c", k=KD)
        wk = w_in[0].rearrange("(k p) c -> p k c", p=P)
        sp_chunk(sp, SPC, [(r[:, :, 64:96], wk[:, :, C_KR:C_KR + 32]),
                           (r[:, :, 96:112], wk[:, :, C_KR + 16:C_KR + 32]),
                           (r[:, :, 112:128], wk[:, :, C_KR:C_KR + 16]),
                           (r[:, :, 0:8], wk[:, :, C_I:C_I + 8]),
                           (r[:, :, 32:40], wk[:, :, C_F:C_F + 8])])
        for j in range(4):
            cols4(sp, MQK + j, w_in, j % 2, C_MQ + 256 * (j // 2))
        for j in range(2):
            r = raw(UQ + j).rearrange("p (k h c) -> p k h c", k=2, h=4)
            q4 = w["mla_w_uq"][0].rearrange("(k p) (h c) -> p k h c", p=P, c=NOPE + ROPE)
            pcs = []
            s = (UQ + j) % RING
            sp.wait_ge(w_lo_done, UQ + j - RING + 1)
            for dst0, c0, c1 in ((0, 0, 96), (96, 80, 96), (112, 64, 80)):
                for k in range(2):
                    pcs.append((r[:, k, :, dst0:dst0 + c1 - c0], q4[:, k, 4 * j:4 * j + 4, c0:c1]))
            for dst, src in pcs:
                sp.dma_start(dst, src).then_inc(w_loaded[s], 16)
        cols2(sp, UK, w["mla_w_uk"], 0, 0)
        cols2(sp, UV, w["mla_w_uv"], 0, 0)
        for j in range(8):
            cols4(sp, GAC + j, w_in, j % 2, C_G + 256 * (j // 2))
        for j in range(4):
            cols2(sp, MV + j, w_in, 256 * j, C_MV)
        for j in range(4):
            cols2(sp, MO + j, w_in, 256 * j, C_MO)
        for j in range(8):
            cols4(sp, GBC + j, w_in, j % 2, C_G + D + 256 * (j // 2))
        for j in range(4):
            cols4(sp, BA + j, w["w_branch_mla"], 0, 256 * j)
        for j in range(4):
            cols4(sp, BB + j, w["w_branch_ml"], 0, 256 * j)
        for j in range(8):
            g, half = (j % 2, j // 2) if j < 4 else (j // 2, j % 2)
            cols4(sp, WO + j, w["w_out"], half, 256 * g)

    MQB = [1, 2, 3, 4]
    QB = [7, 0, 1, 2]
    KVB = [3, 4, 7, 0]
    VB = [1, 2, 3, 4]

    def fm_pair(pe, n, half, banks, a_hi, a_lo, ktiles):
        pe.wait_ge(w_lo_done, n + 1)
        for kk in range(4):
            k = 4 * half + kk
            for f in range(2):
                c = kk * 256 + f * P
                last = three(B[banks[f]][:], wv(n, c, c + P), a_hi[:, k, :], a_lo[:, k, :], k == 0, k == ktiles - 1)
        last.then_inc(w_used, 1)

    def q_padded(hh, c):
        return (mqk if hh % 2 == 0 else tbuf)[:, hh // 2, c * P:(c + 1) * P]

    def mixer_pe(pe):
        lead_pe(pe, 1, CQ)
        pe.wait_ge(w_lo_done, SPC + 1)
        for k in range(KD):
            last = three(B[0][:], wv(SPC, k * P, (k + 1) * P), v_hi[:, k, :], v_lo[:, k, :], k == 0, k == KD - 1)
        last.then_inc(w_used, 1)
        bs[1].wait(pe, "rb_ready", 1)
        fm_pair(pe, MQK, 0, MQB[0:2], v_hi, v_lo, KD)
        pe.wait_ge(ms["cq_sq"], 4)
        for g in range(2):
            for tb in range(TB):
                for f in range(2):
                    last = nc.tensor.matmul(B[5][:, 4 * g + tb:4 * g + tb + 1],
                                            scratch[:, 2 * g + f, tb * P:(tb + 1) * P], ones[:, 0:1],
                                            start=(f == 0), stop=(f == 1))
        last.then_inc(ms["q_sums"], 1)
        fm_pair(pe, MQK + 1, 1, MQB[0:2], v_hi, v_lo, KD)
        fm_pair(pe, MQK + 2, 0, MQB[2:4], v_hi, v_lo, KD)
        pe.wait_ge(ms["rq_ready"], 1)
        bcast_rows(B[6], rq[:, 4:8]).then_inc(ms["rkb_ready"], 1)
        fm_pair(pe, MQK + 3, 1, MQB[2:4], v_hi, v_lo, KD)
        pe.wait_ge(ms["cq_split"], 4)
        for hd in range(HEADS):
            j = UQ + hd // 4
            if hd % 4 == 0:
                pe.wait_ge(w_lo_done, j + 1)
            if hd == 1:
                pe.wait_ge(ms["kr_done"], 1)
            if hd == 2:
                pe.wait_ge(ms["conv_in"], 4)
            if hd >= 4:
                pe.wait_ge(ms["Q_done"], hd - 3)
            for k in range(2):
                c = k * 512 + (hd % 4) * P
                last = three(B[QB[hd % 4]][:], wv(j, c, c + P), cq_hi[:, k, :], cq_lo[:, k, :], k == 0, k == 1)
            if hd % 4 == 3:
                last.then_inc(w_used, 1)
        pe.wait_ge(w_lo_done, UK + 1)
        for pr in range(4):
            if pr == 2:
                pe.wait_ge(ms["Q_done"], 6)
            for k in range(2):
                c = k * 512 + pr * P
                last = three(B[KVB[pr]][:], wv(UK, c, c + P), cq_hi[:, 2 + k, :], cq_lo[:, 2 + k, :], k == 0, k == 1)
        last.then_inc(w_used, 1)
        pe.wait_ge(w_lo_done, UV + 1)
        for tb in range(TB):
            if tb == 0:
                pe.wait_ge(ms["Q_done"], 8)
            if tb == 2:
                pe.wait_ge(ms["K_done"], 4)
            for k in range(2):
                last = three_tm(B[VB[tb]][:], wv(UV, k * 512, (k + 1) * 512), cq_hi[:, 2 + k, tb * P:(tb + 1) * P],
                                cq_lo[:, 2 + k, tb * P:(tb + 1) * P], k == 0, k == 1)
            last.then_inc(ms["v_ps"] if tb < TB - 1 else w_used, 1)
        pe.wait_ge(ms["Q_done"], HEADS)

        def pv(t):
            hh, b = t // 4, t % 4
            pe.wait_ge(ms["pt_even"] if t % 2 == 0 else ms["pt_odd"], t // 2 + 1)
            if b == 0 and hh >= 1:
                pe.wait_ge(ms["o_done"], hh)
            for kb in range(TB):
                last = nc.tensor.matmul(B[7][:, b * VDIM:(b + 1) * VDIM], PT[:, t % 2, kb * P:(kb + 1) * P],
                                        Vm[:, kb, hh * VDIM:(hh + 1) * VDIM], start=(kb == 0), stop=(kb == TB - 1))
            last.then_inc(ms["pv"], 1)

        for hd in range(HEADS + 1):
            for b in range(TB):
                if hd < HEADS:
                    s = 4 * hd + b
                    if b == 0:
                        pe.wait_ge(ms["K_done"], hd + 1)
                    if s < 3:
                        pe.wait_ge(ms["Vm_done"], s + 2)
                    else:
                        pe.wait_ge(ms["exp"], s - 2)
                    nc.tensor.matmul(B[2 + s % 3][:], Q[:, hd, b * P:(b + 1) * P], K[:, hd, :], start=True,
                                     stop=True).then_inc(ms["scores"], 1)
                if hd >= 1:
                    t = 4 * (hd - 1) + b
                    pe.wait_ge(ms["exp"], t + 1)
                    if t >= 2:
                        pe.wait_ge(ms["pt_even"] if t % 2 == 0 else ms["pt_odd"], t // 2)
                    for kb in range(TB):
                        last = nc.tensor.transpose(B[5 + t % 2][:, kb * P:(kb + 1) * P],
                                                   Pm[:, b, kb * P:(kb + 1) * P], ident[:])
                    last.then_inc(ms["pT"], 1)
                    if t >= 1:
                        pv(t - 1)
            if hd < HEADS:
                if hd % 2 == 0 and hd >= 2:
                    pe.wait_ge(ms["ga"], hd)
                fm_pair(pe, GAC + hd, hd % 2, [0, 1], v_hi, v_lo, KD)
        pv(4 * HEADS - 1)
        MVB, MOB = [2, 3, 4, 7], [0, 1, 5, 6]
        for j in range(4):
            if j == 0:
                pe.wait_ge(ms["o_done"], HEADS)
            if j >= 2:
                pe.wait_ge(ms["oT_split"], j - 1)
            for tb in range(TB):
                last = nc.tensor.transpose(B[5 + j % 2][:, tb * P:(tb + 1) * P], O[:, tb, j * P:(j + 1) * P], ident[:])
            last.then_inc(ms["oTT"], 1)
        def tm_chunk(n0, j, banks):
            pe.wait_ge(w_lo_done, n0 + j + 1)
            for kk in range(2):
                k = 2 * j + kk
                for tb in range(TB):
                    last = three_tm(B[banks[tb]][:], wv(n0 + j, kk * 512, (kk + 1) * 512),
                                    v_hi[:, k, tb * P:(tb + 1) * P], v_lo[:, k, tb * P:(tb + 1) * P],
                                    k == 0, k == KD - 1)
            last.then_inc(w_used, 1)

        for j in range(4):
            tm_chunk(MV, j, MVB)
        pe.wait_ge(ms["ga"], 8)
        pe.wait_ge(ms["oT_split"], 4)
        tm_chunk(MO, 0, MOB)
        tm_chunk(MO, 1, MOB)
        pe.wait_ge(ms["Vml"], TB)
        for d in range(2):
            pe.wait_ge(ms["rows"], d + 1)
            for c in range(TB):
                last = nc.tensor.transpose(B[2 + d][:, c * P:(c + 1) * P], scratch[:, d, c * P:(c + 1) * P], ident[:])
            last.then_inc(ms["RQ_T"], 1)
        pe.wait_ge(ms["mqk_done"], 6)
        for pr in range(2):
            for c in range(TB):
                last = nc.tensor.transpose(B[4 + 3 * pr][:, c * P:(c + 1) * P], mqk[:, 2 + pr, c * P:(c + 1) * P], ident[:])
            last.then_inc(ms["kT_T"], 1)
        tm_chunk(MO, 2, MOB)
        for d in range(2):
            pe.wait_ge(ms["D8"], d + 1)
            if d == 0:
                pe.wait_ge(ms["cx"], 4)
            last = nc.tensor.matmul(B[3][:, 32 * d:32 * d + 32], ones[0:8, :], D8[d][0:8, :], start=True, stop=True)
        last.then_inc(ms["decb_ps"], 1)
        tm_chunk(MO, 3, MOB)
        units = UNITS
        pe.wait_ge(ms["cx"], 4)
        pe.wait_ge(ms["K_tm"], 2)
        pe.wait_ge(ms["decb"], 4)

        def mb(u):
            d, c = units[u]
            if u >= 1:
                pe.wait_ge(ms["Ebig"], 4 * u)
                pe.wait_ge(ms["Sm"], u)
            for hh in range(MLH):
                r = 32 * d + 4 * d + hh
                last = nc.tensor.matmul(B[2][:, hh * P:(hh + 1) * P],
                                        ident[32 * d:32 * d + 8, r:r + 1].broadcast_to([8, P]),
                                        Mrows[32 * d:32 * d + 8, c * P:(c + 1) * P], start=True, stop=True)
            last.then_inc(ms["Mb"], 1)
            for hh in range(MLH):
                last = nc.tensor.matmul(B[7][:, hh * P:(hh + 1) * P], mqk[:, 2 + hh // 2, c * P:(c + 1) * P],
                                        q_padded(hh, c), start=True, stop=True)
            last.then_inc(ms["QK"], 1)

        pe.wait_ge(ms["q_split"], 6)
        mb(0)
        for u in range(8):
            d, c = units[u]
            if u % 2 == 0:
                if u >= 2:
                    pe.wait_ge(ms["gb"], u)
                else:
                    pe.wait_ge(ms["mo"], TB)
            fm_pair(pe, GBC + u, u % 2, [0, 1], v_hi, v_lo, KD)
            if u < 7:
                mb(u + 1)
            first, final = u < 2, u >= 6
            pe.wait_ge(ms["Sm"], u + 1)
            if not final:
                pe.wait_ge(ms["Kp"], u + 1)
            if u >= 1:
                pe.wait_ge(ms["den"], u)
                pe.wait_ge(ms["Cnew"], 6 * min(u, 6))
            for hh in range(MLH):
                nc.tensor.matmul(B[3][:, hh * P:(hh + 1) * P], scratch[:, u % 2, hh * P:(hh + 1) * P],
                                 V[:, c, hh * P:(hh + 1) * P], start=True, stop=True)
                last = nc.tensor.matmul(B[6][:, 64 + hh:65 + hh], scratch[:, u % 2, hh * P:(hh + 1) * P], ones[:, 0:1],
                                        start=True, stop=True)
            if not first:
                for hh in range(MLH):
                    pr, q = hh // 2, q_padded(hh, c)
                    nc.tensor.matmul(B[4][:, hh * P:(hh + 1) * P], q, C[:, d, pr, :], start=True, stop=True)
                    last = nc.tensor.matmul(B[6][:, 68 + hh:69 + hh], q, nstate[:, 2 * d + pr:2 * d + pr + 1],
                                            start=True, stop=True)
            kp = [sqacc[:, 256 * (u % 2) + P * pr:256 * (u % 2) + P * (pr + 1)] for pr in range(2)]
            if not final:
                for pr in range(2):
                    last = nc.tensor.matmul(B[6][:, 72 + pr:73 + pr], kp[pr], ones[:, 0:1], start=True, stop=True)
            last.then_inc(ms["num"], 1)
            if not final:
                for pr in range(2):
                    last = nc.tensor.matmul(B[5][:, 256 * pr:256 * pr + 256], kp[pr], V[:, c, 256 * pr:256 * pr + 256],
                                            start=True, stop=True)
                last.then_inc(ms["Cps"], 1)
        pe.wait_ge(ms["gb"], 8)
        for g in range(4):
            if g == 2:
                pe.wait_ge(ms["den"], 8)
            if g == 3:
                pe.wait_ge(ms["GM"], 2)
            fm_pair(pe, BA + g, 0, BAB[g], oT_hi, oT_lo, 4)
        pe.wait_ge(ms["hn"], 16)
        for j in range(4):
            if j == 2:
                pe.wait_ge(ms["GM"], 4)
            for tb in range(TB):
                last = nc.tensor.transpose(B[BTB[j]][:, tb * P:(tb + 1) * P], HS[:, tb, j * P:(j + 1) * P], ident[:])
            last.then_inc(ms["bTT"], 1)
        pe.wait_ge(ms["bT_split"], 4)
        for g in range(4):
            if g < 2:
                pe.wait_ge(ms["GM"], 2 * g + 6)
            if g == 3:
                pe.wait_ge(ms["b_out"], 4)
            fm_pair(pe, BB + g, 0, BBB[g], bT_hi, bT_lo, 4)
        pe.wait_ge(ms["b_out"], 4)
        for j in range(8):
            g, half = (j % 2, j // 2) if j < 4 else (j // 2, j % 2)
            if j % 2 == 0 and j < 4:
                pe.wait_ge(ms["mixed"], 2 * j + 4)
            fm_pair(pe, WO + j, half, [YBANK[2 * g], YBANK[2 * g + 1]], v_hi, v_lo, KD)

    BAB = [(2, 7), (0, 1), (5, 6), (2, 7)]
    BTB = [3, 4, 0, 1]
    BBB = [(5, 6), (7, 2), (0, 1), (3, 2)]

    UNITS = [(0, 0), (1, 3), (0, 1), (1, 2), (0, 2), (1, 1), (0, 3), (1, 0)]

    def conv_tile(dve, ct):
        o = mqk[:, ct, :]
        wc = VEC["ml_conv_w"]
        for j in range(CONV):
            sc = cols[:, wc + 4 * j + ct:wc + 4 * j + ct + 1]
            src = conv_in[:, ct, j:j + S]
            if j == 0:
                ins = nc.vector.tensor_scalar(o, src, sc, None, ALU.mult)
            else:
                ins = nc.vector.scalar_tensor_tensor(o, src, sc, o, ALU.mult, ALU.add)
            if j < CONV - 1:
                dlink(dve, ins)
            else:
                ins.then_inc(ms["conv_done"], 1)

    def v4(ap):
        return ap.rearrange("p (a b) -> p a b", a=4)

    def mixer_dve(dve):
        lead_dve(dve, 1, CQ)
        dlink(dve, nc.vector.memset(conv_in[:, :, 0:2], 0.0))
        dlink(dve, nc.vector.memset(conv_in[:, :, S + 2:S + 4], 0.0))
        for t in range(4):
            dve_after(dve, CQ + 2 + t // 2)
            nc.vector.tensor_tensor(cq_t[:, t, :], B[4 + t][:], r_b[:], ALU.mult).then_inc(ms["cq_t"], 1)
        for t in range(4):
            dve.wait_ge(ms["cq_t"], t + 1)
            dve.wait_ge(ms["cq_hi"], t + 1)
            g = col("mla_q_norm", t) if t < 2 else col("mla_kv_norm", t - 2)
            nc.vector.scalar_tensor_tensor(cq_lo[:, t, :], cq_t[:, t, :], g, cq_hi[:, t, :].bitcast(F32), ALU.mult,
                                           ALU.subtract).then_inc(ms["cq_split"], 1)
        dve.wait_ge(bias_in, 32)
        dve_after(dve, SPC)
        dlink(dve, nc.vector.tensor_tensor(i_row, B[0][0:8, :], r_b[0:8, :], ALU.mult))
        dlink(dve, nc.vector.tensor_scalar(i_row, i_row, ifb[0:8, 0:1], None, ALU.add))
        dlink(dve, nc.vector.tensor_tensor(lf_row, B[0][32:40, :], r_b[32:40, :], ALU.mult))
        dlink(dve, nc.vector.tensor_scalar(lf_row, lf_row, ifb[0:8, 1:2], None, ALU.add))
        dve.wait_ge(ms["q_sums"], 1)
        x = scratch[0:8, 2, :]
        nc.vector.scalar_tensor_tensor(x, lf_row, -1.0, lf_row, ALU.mult, ALU.max).then_inc(ms["f_abs"], 1)
        t0, t1 = scratch[:, 0, :], scratch[:, 1, :]
        dlink(dve, nc.vector.tensor_tensor(t0[64:128, :], B[0][64:128, :], r_b[64:128, :], ALU.mult))
        dlink(dve, nc.vector.tensor_tensor(t0[64:128, :], t0[64:128, :], CS[64:128, :], ALU.mult))
        dlink(dve, nc.vector.tensor_copy(t1[64:96, :], t0[96:128, :]))
        dlink(dve, nc.vector.tensor_tensor(t0[64:96, :], t0[64:96, :], t1[64:96, :], ALU.add))
        rsqrt(dve, rq, B[5][:, 0:8], 8, 1.0 / RANK).then_inc(ms["rq_ready"], 1)
        dlink(dve, nc.vector.tensor_copy(K[64:96, :, :], t0[64:96, None, :].broadcast_to([32, HEADS, S])))
        nc.vector.tensor_copy(K[96:128, :, :], t0[64:96, None, :].broadcast_to([32, HEADS, S])).then_inc(ms["kr_done"], 1)
        dve.wait_ge(ms["rq_ready"], 1)
        dlink(dve, nc.vector.tensor_scalar(rqs, rq[:, 0:4], SCALE, None, ALU.mult))
        dve.wait_ge(ms["f_ln"], 1)
        dlink(dve, nc.vector.scalar_tensor_tensor(lf_row, lf_row, 0.0, x, ALU.min, ALU.subtract))
        for ct in range(4):
            dve_after(dve, MQK + 1 + 2 * (ct // 2))
            nc.vector.tensor_tensor(conv_in[:, ct, 2:S + 2], B[MQB[ct]][:], r_b[:], ALU.mult).then_inc(ms["conv_in"], 1)
        dve.wait_ge(ms["rkb_ready"], 1)
        rkb = scratch[:, 3, :]
        nc.vector.tensor_copy(rkb, B[6][:]).then_inc(ms["rkb_copied"], 1)
        for hd in range(HEADS):
            dve_after(dve, UQ + hd // 4)
            nc.vector.tensor_tensor(Q[:, hd, :], B[QB[hd % 4]][:], CS[:], ALU.mult).then_inc(ms["Q_done"], 1)
        dve.wait_ge(ms["rkb_copied"], 1)
        dve_after(dve, UK)
        for hd in range(HEADS):
            r0 = 64 * (hd % 2)
            nc.vector.tensor_tensor(K[0:64, hd, :], B[KVB[hd // 2]][r0:r0 + 64, :], rkb[r0:r0 + 64, :],
                                    ALU.mult).then_inc(ms["K_done"], 1)
        def o_out(hh):
            dve.wait_ge(ms["exp"], 4 * hh + 4)
            dlink(dve, nc.vector.reciprocal(rsum, sums[:, 4 * hh:4 * hh + 4]))
            dve.wait_ge(ms["pv"], 4 * hh + 4)
            nc.vector.tensor_tensor(O[:, :, hh * VDIM:(hh + 1) * VDIM],
                                    B[7][:, 0:4 * VDIM].rearrange("p (b v) -> p b v", b=4),
                                    rsum[:, :, None].broadcast_to([P, TB, VDIM]), ALU.mult).then_inc(ms["o_done"], 1)
            dve.wait_ge(ms["o_done"], hh + 1)

        def ga_out(g):
            dve_after(dve, GAC + 2 * g + 1)
            for f in range(2):
                nc.vector.tensor_tensor(gates_a[:, 2 * g + f, :], B[f][:], r_b[:], ALU.mult).then_inc(ms["ga"], 1)

        for hd in range(HEADS + 1):
            for b in range(TB):
                if hd < HEADS:
                    s = 4 * hd + b
                    dve.wait_ge(ms["scores"], s + 1)
                    if s >= 4:
                        dve.wait_ge(ms["exp"], s - 3)
                    dlink(dve, nc.vector.tensor_reduce(mx[:, b:b + 1], B[2 + s % 3][:], AX.X, ALU.max))
                    nc.vector.tensor_scalar(nb[:, b:b + 1], mx[:, b:b + 1], rqs[:, b:b + 1], -1.0, ALU.mult,
                                            ALU.mult).then_inc(ms["nb"], 1)
                if hd >= 2 and b == 0:
                    o_out(hd - 2)
                if hd % 2 == 0 and hd >= 2 and b == 1:
                    ga_out(hd // 2 - 1)
                if hd >= 1 and b % 2 == 1:
                    t = 4 * (hd - 1) + b
                    dve.wait_ge(ms["pT"], t + 1)
                    nc.vector.tensor_copy(PT[:, 1, :], B[6][:]).then_inc(ms["pt_odd"], 1)
            if hd < HEADS:
                lo_upto(dve, GAC + hd + 3)
                if 1 <= hd <= 4:
                    conv_tile(dve, hd - 1)
        o_out(HEADS - 1)
        for j in range(4):
            dve.wait_ge(ms["oT_hi"], j + 1)
            nc.vector.tensor_tensor(oT_lo[:, j, :], B[5 + j % 2][:], oT_hi[:, j, :].bitcast(F32),
                                    ALU.subtract).then_inc(ms["oT_split"], 1)
        bb, dd, M = scratch[0:8, 2, :], scratch[0:8, 3, :], sqacc[0:8, :]
        for d in range(2):
            def rv(ap):
                return ap if d == 0 else ap[:, ::-1]
            RQ = scratch[:, d, :]
            dlink(dve, nc.vector.memset(RQ, 0.0))
            dlink(dve, nc.vector.memset(dd, 1.0))
            dlink(dve, nc.vector.memset(dd[:, 0:S:P] if d == 0 else dd[:, P - 1:S:P], 0.0))
            dlink(dve, nc.vector.tensor_tensor_scan(rv(bb), rv(dd), rv(lf_row), 0.0, ALU.mult, ALU.add))
            dlink(dve, nc.vector.tensor_tensor(RQ[0:8, :], i_row, bb, ALU.subtract))
            dlink(dve, nc.vector.memset(dd, 0.0))
            ends = bb[:, P - 1:S - 1:P] if d == 0 else bb[:, P:S:P]
            dlink(dve, nc.vector.tensor_copy(dd[:, P:S:P] if d == 0 else dd[:, P - 1:S - 1:P], ends))
            dlink(dve, nc.vector.tensor_tensor_scan(rv(M), rv(dd), rv(RQ[0:8, :]), 0.0, ALU.add, ALU.max))
            dlink(dve, nc.vector.tensor_copy(Mrows[32 * d:32 * d + 8, :], M))
            dlink(dve, nc.vector.memset(mc[d][0:8, :], 0.0))
            if d == 0:
                dlink(dve, nc.vector.tensor_tensor(mc[d][0:8, 1:4], M[:, P - 1:S - 1:P], bb[:, P - 1:S - 1:P], ALU.add))
                mlast = M[:, P - 1:S:P]
            else:
                dlink(dve, nc.vector.tensor_tensor(mc[d][0:8, 0:3], M[:, P:S:P], bb[:, P:S:P], ALU.add))
                mlast = M[:, 0:S:P]
            lo_upto(dve, MV + 3 + 2 * d)
            nc.vector.tensor_tensor(dcy[d][0:8, :], mc[d][0:8, :], mlast, ALU.subtract).then_inc(ms["dcy"], 1)
            dlink(dve, nc.vector.tensor_tensor(v4(RQ[32:40, :]), mc[d][0:8, :, None].broadcast_to([8, TB, P]), v4(M),
                                               ALU.subtract))
            dlink(dve, nc.vector.scalar_tensor_tensor(RQ[64:72, :], bb, -1.0, M, ALU.mult, ALU.subtract))
            nc.vector.tensor_tensor(v4(RQ[96:104, :]), v4(RQ[0:8, :]),
                                    mlast[:, :, None].broadcast_to([8, TB, P]), ALU.subtract).then_inc(ms["rows"], 1)
            dve.wait_ge(ms["rows"], d + 1)
        lo_upto(dve, MO + 3)
        for d in range(2):
            dve.wait_ge(ms["dexp"], d + 1)
            nc.vector.tensor_tensor(D8[d][0:8, :].rearrange("p (c r) -> p c r", c=4),
                                    ident[0:8, None, 0:8].broadcast_to([8, 4, 8]),
                                    dcy[d][0:8, :, None].broadcast_to([8, 4, 8]), ALU.mult).then_inc(ms["D8"], 1)
        dve.wait_ge(masks_made, 2)
        dve.wait_ge(ms["cx"], 4)
        lo_upto(dve, GBC + 2)

        def ebig(u):
            d, c = UNITS[u]
            dve.wait_ge(ms["Mb"], u + 1)
            if u >= 2:
                dve.wait_ge(ms["num"], u - 1)
            for hh in range(MLH):
                nc.vector.scalar_tensor_tensor(scratch[:, u % 2, hh * P:(hh + 1) * P], B[2][:, hh * P:(hh + 1) * P],
                                               cx[:, d, c, 0, 4 * d + hh:4 * d + hh + 1], maskbig[:, d, :],
                                               ALU.subtract, ALU.max).then_inc(ms["Ebig"], 1)

        def gb_out(g):
            dve_after(dve, GBC + 2 * g + 1)
            for f in range(2):
                nc.vector.tensor_tensor(gates_b[:, 2 * g + f, :], B[f][:], r_b[:], ALU.mult).then_inc(ms["gb"], 1)

        ebig(0)
        for u in range(8):
            d, c = UNITS[u]
            dve.wait_ge(ms["Eexp"], u + 1)
            dve.wait_ge(ms["QK"], u + 1)
            nc.vector.tensor_tensor(scratch[:, u % 2, :], scratch[:, u % 2, :], B[7][:], ALU.mult).then_inc(ms["Sm"], 1)
            lo_upto(dve, GBC + u + 3)
            if u < 7:
                ebig(u + 1)
            if u % 2 == 1:
                gb_out(u // 2)
            dve.wait_ge(ms["num"], u + 1)
            if u >= 2:
                dve.wait_ge(ms["hs"], u - 1)
            tmp, dn4 = scratch[:, 2 + u % 2, :], den[:, 4 * (u % 2):4 * (u % 2) + 4]
            inter = cx[:, d, c, 1, 4 * d:4 * d + 4]
            floor = cx[:, d, c, 2, 4 * d:4 * d + 4]
            if u < 2:
                dlink(dve, nc.vector.tensor_copy(tmp, B[3][:]))
                dlink(dve, nc.vector.tensor_copy(dn4, B[6][:, 64:68]))
            else:
                dlink(dve, nc.vector.tensor_tensor(v4(tmp), v4(B[4][:]), inter[:, :, None].broadcast_to([P, MLH, P]),
                                                   ALU.mult))
                dlink(dve, nc.vector.tensor_tensor(tmp, tmp, B[3][:], ALU.add))
                dlink(dve, nc.vector.tensor_tensor(dn4, B[6][:, 68:72], inter, ALU.mult))
                dlink(dve, nc.vector.tensor_tensor(dn4, dn4, B[6][:, 64:68], ALU.add))
            dlink(dve, nc.vector.scalar_tensor_tensor(dn4, dn4, -1.0, dn4, ALU.mult, ALU.max))
            dlink(dve, nc.vector.tensor_tensor(dn4, dn4, floor, ALU.max))
            nc.vector.reciprocal(dn4, dn4).then_inc(ms["den"], 1)
            if u < 6:
                dve.wait_ge(ms["Cps"], u + 1)
                for hh in range(MLH):
                    b0, pr = 64 * (hh % 2), hh // 2
                    src = B[5][b0:b0 + 64, 256 * pr + P * (hh % 2):256 * pr + P * (hh % 2) + P]
                    st = C[b0:b0 + 64, d, pr, :]
                    if u < 2:
                        nc.vector.tensor_copy(st, src).then_inc(ms["Cnew"], 1)
                    else:
                        dc = decb[b0:b0 + 64, 8 * d + 2 * c + pr:8 * d + 2 * c + pr + 1]
                        nc.vector.scalar_tensor_tensor(st, st, dc, src, ALU.mult, ALU.add).then_inc(ms["Cnew"], 1)
                for pr in range(2):
                    st = nstate[:, 2 * d + pr:2 * d + pr + 1]
                    if u < 2:
                        nc.vector.tensor_copy(st, B[6][:, 72 + pr:73 + pr]).then_inc(ms["Cnew"], 1)
                    else:
                        dc = decb[:, 8 * d + 2 * c + pr:8 * d + 2 * c + pr + 1]
                        nc.vector.scalar_tensor_tensor(st, st, dc, B[6][:, 72 + pr:73 + pr], ALU.mult,
                                                       ALU.add).then_inc(ms["Cnew"], 1)
                dve.wait_ge(ms["Cnew"], 6 * (u + 1))
        def gate_mla(g):
            dve_after(dve, BA + g)
            for f in range(2):
                m = 2 * g + f
                dve.wait_ge(ms["ga_sig"], m + 1)
                nc.vector.tensor_tensor(gates_a[:, m, :], B[BAB[g][f]][:], gates_a[:, m, :], ALU.mult).then_inc(ms["GM"], 1)

        gate_mla(0)
        dve.wait_ge(ms["hn_sq"], 16)
        dve.wait_ge(ms["og"], TB)
        dlink(dve, rsqrt(dve, hrs, hsq, 16, 1.0 / MLV))
        for tb in range(TB):
            for hh in range(MLH):
                o = HS[:, tb, hh * P:(hh + 1) * P]
                last = nc.vector.scalar_tensor_tensor(o, o, hrs[:, 4 * tb + hh:4 * tb + hh + 1],
                                                      og[:, tb, hh * P:(hh + 1) * P], ALU.mult, ALU.mult)
                last.then_inc(ms["hn"], 1)
        gate_mla(1)
        gate_mla(2)
        for j in range(4):
            dve.wait_ge(ms["bT_hi"], j + 1)
            nc.vector.scalar_tensor_tensor(bT_lo[:, j, :], B[BTB[j]][:], col("ml_head_norm", j),
                                           bT_hi[:, j, :].bitcast(F32), ALU.mult, ALU.subtract).then_inc(ms["bT_split"], 1)
        gate_mla(3)

        def mix_lo(m):
            dve.wait_ge(ms["mixhi"], m + 1)
            nc.vector.tensor_tensor(v_lo[:, m, :], gates_b[:, m, :], v_hi[:, m, :].bitcast(F32),
                                    ALU.subtract).then_inc(ms["mixed"], 1)
        for g in range(4):
            dve_after(dve, BB + g)
            for f in range(2):
                m = 2 * g + f
                dve.wait_ge(ms["gb_sig"], m + 1)
                nc.vector.tensor_tensor(gates_b[:, m, :], B[BBB[g][f]][:], gates_b[:, m, :], ALU.mult).then_inc(ms["b_out"], 1)
                dve.wait_ge(ms["b_out"], m + 1)
                nc.vector.tensor_tensor(gates_b[:, m, :], gates_a[:, m, :], gates_b[:, m, :],
                                        ALU.add).then_inc(ms["mx_t"], 1)
                dve.wait_ge(ms["mx_t"], m + 1)
                if m >= 1:
                    mix_lo(m - 1)
        mix_lo(7)

    def mixer_act(act):
        lead_act(act, 1, CQ)
        bs[1].wait(act, "h_acc", KD)
        for t in range(4):
            hi_upto(act, CQ + 4 + 2 * (t // 2))
            act.wait_ge(ms["cq_t"], t + 1)
            g = col("mla_q_norm", t) if t < 2 else col("mla_kv_norm", t - 2)
            nc.scalar.activation(cq_hi[:, t, :], cq_t[:, t, :], ACT.Copy, scale=g).then_inc(ms["cq_hi"], 1)
            nc.scalar.activation(scratch[:, t, :], cq_t[:, t, :], ACT.Square).then_inc(ms["cq_sq"], 1)
        hi_upto(act, SPC + 3)
        act.wait_ge(ms["f_abs"], 1)
        x = scratch[0:8, 2, :]
        alink(act, nc.scalar.activation(x, x, ACT.Exp, scale=-1.0))
        nc.scalar.activation(x, x, ACT.Ln, bias=1.0).then_inc(ms["f_ln"], 1)
        hi_upto(act, UV + 3)
        for tb in range(TB):
            if tb < TB - 1:
                act.wait_ge(ms["v_ps"], tb + 1)
            else:
                act.wait_ge(w_used, UV + 1)
            nc.scalar.activation(Vm[:, tb, :], B[VB[tb]][:], ACT.Copy, scale=rq[:, 4 + tb:5 + tb]).then_inc(ms["Vm_done"], 1)
        for hd in range(HEADS + 1):
            for b in range(TB):
                t = 4 * (hd - 1) + b
                if hd >= 1:
                    act.wait_ge(ms["pT"], t + 1)
                if hd < HEADS:
                    s = 4 * hd + b
                    act.wait_ge(ms["nb"], s + 1)
                    nc.scalar.activation(Pm[:, b, :], B[2 + s % 3][:], ACT.Exp, bias=nb[:, b:b + 1],
                                         scale=rqs[:, b:b + 1], accum_out=sums[:, s:s + 1]).then_inc(ms["exp"], 1)
                if hd >= 1 and b % 2 == 0:
                    nc.scalar.activation(PT[:, 0, :], B[5][:], ACT.Copy).then_inc(ms["pt_even"], 1)
            if hd < HEADS:
                hi_upto(act, GAC + hd + 3)
        for j in range(4):
            act.wait_ge(ms["oTT"], j + 1)
            nc.scalar.activation(oT_hi[:, j, :], B[5 + j % 2][:], ACT.Copy).then_inc(ms["oT_hi"], 1)
        for m in range(8):
            act.wait_ge(ms["ga"], m + 1)
            nc.scalar.activation(gates_a[:, m, :], gates_a[:, m, :], ACT.Sigmoid).then_inc(ms["ga_sig"], 1)
        hi_upto(act, MV + 2)
        for ct in range(4):
            act.wait_ge(ms["conv_done"], ct + 1)
            nc.scalar.activation(mqk[:, ct, :], mqk[:, ct, :], ACT.Silu,
                                 bias=col("ml_conv_b", ct)).then_inc(ms["mqk_done"], 1)
        act_after(act, MV + 3)
        for tb in range(TB):
            nc.scalar.activation(V[:, tb, :], B[[2, 3, 4, 7][tb]][:], ACT.Copy, scale=rc[:, tb:tb + 1]).then_inc(ms["Vml"], 1)
        for d in range(2):
            act.wait_ge(ms["dcy"], d + 1)
            nc.scalar.activation(dcy[d][0:8, :], dcy[d][0:8, :], ACT.Exp).then_inc(ms["dexp"], 1)
        hi_upto(act, MO + 3)
        for d in range(2):
            act.wait_ge(ms["RQ_T"], d + 1)
            src = B[2 + d][:].rearrange("p (c q r) -> p c q r", c=4, q=4)
            nc.scalar.activation(cx[:, d, :, 0, :], src[:, :, 0, 0:8], ACT.Copy).then_inc(ms["cx"], 1)
            nc.scalar.activation(cx[:, d, :, 1:4, :], src[:, :, 1:4, 0:8], ACT.Exp).then_inc(ms["cx"], 1)
        for pr in range(2):
            act.wait_ge(ms["kT_T"], pr + 1)
            nc.scalar.activation(K_tm[:, :, pr * P:(pr + 1) * P], v4(B[4 + 3 * pr][:]), ACT.Copy).then_inc(ms["K_tm"], 1)
        act.wait_ge(ms["decb_ps"], 1)
        for d in range(2):
            for par in range(2):
                r = slice(64 * par, 64 * par + 64)
                src = B[3][r, 32 * d:32 * d + 32].rearrange("p (c r) -> p c r", c=4)[:, :, 4 * d + par:4 * d + par + 3:2]
                nc.scalar.activation(decb[r, 8 * d:8 * d + 8].rearrange("p (c r) -> p c r", c=4), src,
                                     ACT.Copy).then_inc(ms["decb"], 1)
        act_after(act, MO + 3)
        for tb in range(TB):
            nc.scalar.activation(og[:, tb, :], B[[0, 1, 5, 6][tb]][:], ACT.Copy,
                                 scale=rc[:, tb:tb + 1]).then_inc(ms["mo"], 1)
        for u in range(8):
            act.wait_ge(ms["Ebig"], 4 * u + 4)
            nc.scalar.activation(scratch[:, u % 2, :], scratch[:, u % 2, :], ACT.Exp, scale=-1.0).then_inc(ms["Eexp"], 1)
            hi_upto(act, GBC + u + 3)
        hi_upto(act, GBC + 10)
        for tb in range(TB):
            act.wait_ge(ms["mo"], TB)
            nc.scalar.activation(og[:, tb, :], og[:, tb, :], ACT.Sigmoid).then_inc(ms["og"], 1)

        def head_squares(i):
            act.wait_ge(ms["hs"], 5 + i)
            tb = HN_ORDER[i]
            if i == 0:
                act.wait_ge(ms["Kp"], 6)
            for hh in range(MLH):
                squares = (K_tm[:, 2 * i + hh // 2, (hh % 2) * P:(hh % 2) * P + P] if i < 2 else
                           (hn_junk[:] if i == 2 else scratch[:, 3, :])[:, hh * P:(hh + 1) * P])
                nc.scalar.activation(squares, HS[:, tb, hh * P:(hh + 1) * P], ACT.Square,
                                     accum_out=hsq[:, 4 * tb + hh:4 * tb + hh + 1]).then_inc(ms["hn_sq"], 1)

        def gb_sigmoid(m):
            act.wait_ge(ms["gb"], m + 1)
            nc.scalar.activation(gates_b[:, m, :], gates_b[:, m, :], ACT.Sigmoid).then_inc(ms["gb_sig"], 1)

        for i in range(3):
            head_squares(i)
        for m in range(4):
            gb_sigmoid(m)
        head_squares(3)
        for m in range(4, 8):
            gb_sigmoid(m)
        hi_upto(act, BA + 6)
        for j in range(4):
            act.wait_ge(ms["bTT"], j + 1)
            nc.scalar.activation(bT_hi[:, j, :], B[BTB[j]][:], ACT.Copy,
                                 scale=col("ml_head_norm", j)).then_inc(ms["bT_hi"], 1)
        for m in range(8):
            hi_upto(act, BB + 3 + m // 2)
            act.wait_ge(ms["mx_t"], m + 1)
            nc.scalar.activation(v_hi[:, m, :], gates_b[:, m, :], ACT.Copy).then_inc(ms["mixhi"], 1)

    HN_ORDER = [c for _, c in UNITS[4:]]

    def mixer_pool(pool):
        for ct in (2, 3):
            pool.wait_ge(ms["mqk_done"], 4)
            nc.gpsimd.tensor_scalar(mqk[:, ct, :], mqk[:, ct, :], float(MLQK ** -0.5), None, ALU.mult).then_inc(ms["mqk_done"], 1)
        pool.wait_ge(ms["rows"], 2)
        pool.wait_ge(ms["mqk_done"], 6)
        for ct in range(2):
            nc.gpsimd.tensor_copy(tbuf[64:128, ct, :], mqk[64:128, ct, :]).then_inc(ms["q_split"], 1)
            pool.wait_ge(ms["q_split"], 3 * ct + 1)
            nc.gpsimd.memset(tbuf[0:64, ct, :], 0.0).then_inc(ms["q_split"], 1)
            pool.wait_ge(ms["q_split"], 3 * ct + 2)
            nc.gpsimd.memset(mqk[64:128, ct, :], 0.0).then_inc(ms["q_split"], 1)
            pool.wait_ge(ms["q_split"], 3 * ct + 3)
        pool.wait_ge(ms["cx"], 4)
        pool.wait_ge(ms["K_tm"], 2)
        for u in range(9):
            if u < 6:
                d, c = UNITS[u]
                if u >= 2:
                    pool.wait_ge(ms["Cps"], u - 1)
                nc.gpsimd.tensor_tensor(v4(sqacc[:, 256 * (u % 2):256 * (u % 2) + 256]), v4(K_tm[:, c, :]),
                                        cx[:, d, c, 3, 4 * d:4 * d + 4][:, :, None].broadcast_to([P, MLH, MLQK]),
                                        ALU.mult).then_inc(ms["Kp"], 1)
            if u >= 1:
                x = u - 1
                d, c = UNITS[x]
                pool.wait_ge(ms["den"], x + 1)
                tmp = v4(scratch[:, 2 + x % 2, :])
                rd = den[:, 4 * (x % 2):4 * (x % 2) + 4][:, :, None].broadcast_to([P, MLH, P])
                if x < 4:
                    nc.gpsimd.tensor_tensor(v4(HS[:, c, :]), tmp, rd, ALU.mult).then_inc(ms["hs"], 1)
                else:
                    plink(pool, nc.gpsimd.tensor_tensor(tmp, tmp, rd, ALU.mult))
                    pool.wait_ge(ms["hs"], 4)
                    nc.gpsimd.tensor_tensor(HS[:, c, :], HS[:, c, :], scratch[:, 2 + x % 2, :], ALU.add).then_inc(ms["hs"], 1)

    def y_wo(after):
        return lambda eng, p: after(eng, WO + (2 + p // 2 if p < 4 else 2 * (p // 2) + 1))

    ps = Signals("ple")
    EB = [[5, 6, 7, 1], [2, 3, 7, 1]]

    def p_transposes_pe(pe):
        pe.wait_ge(p_in, 32)
        bs[3].wait(pe, "ysq_dve", 1)
        bs[3].wait(pe, "ysq_act", 2)
        for k in range(2):
            for tb in range(TB):
                last = nc.tensor.transpose(B[EB[0][k]][:, tb * P:(tb + 1) * P],
                                           p_tm[tb // 2][:, tb % 2, k * P:(k + 1) * P], ident[:])
            last.then_inc(ps["pT"], 1)

    def e_product_pe(pe, i):
        if i == 0:
            pe.wait_ge(ps["pT_split"], 2)
        pe.wait_ge(w_lo_done, EP + i + 1)
        for q in range(4):
            if i == 1 and q == 2:
                pe.wait_ge(ps["e_out"], 4)
            for k in range(2):
                c = k * 512 + q * P
                last = three(B[EB[i][q]][:], wv(EP + i, c, c + P), pT_hi[:, k, :], pT_lo[:, k, :], k == 0, k == 1)
        last.then_inc(w_used, 1)

    def pT_act(act):
        for k in range(2):
            act.wait_ge(ps["pT"], k + 1)
            nc.scalar.activation(pT_hi[:, k, :], B[EB[0][k]][:], ACT.Copy).then_inc(ps["pT_hi"], 1)

    def pT_dve(dve):
        for k in range(2):
            dve.wait_ge(ps["pT_hi"], k + 1)
            nc.vector.tensor_tensor(pT_lo[:, k, :], B[EB[0][k]][:], pT_hi[:, k, :].bitcast(F32),
                                    ALU.subtract).then_inc(ps["pT_split"], 1)

    def e_act(act, i):
        hi_upto(act, EP + i + 3)
        act.wait_ge(w_used, EP + i + 1)
        for q in range(4):
            nc.scalar.activation(e_sb[:, 4 * i + q, :], B[EB[i][q]][:], ACT.Copy).then_inc(ps["e_out"], 1)

    GB = [4, 5, 6, 7, 2, 3, 0, 1]
    TBANK = [[4, 5, 6, 7], [0, 1, 2, 4]]
    SUMS = 3
    HB = [0, 1, 0, 1, 4, 5, 6, 7]

    def gate_pe(pe):
        def h_pair(g):
            if g == 1:
                pe.wait_ge(ps["hT_out"], 2)
            if g >= 2:
                pe.wait_ge(ps["g_scaled"], 2 * (g - 1))
            for f in range(2):
                m = 2 * g + f
                for tb in range(TB):
                    last = nc.tensor.transpose(B[HB[m]][:, tb * P:(tb + 1) * P], h[:, m, tb * P:(tb + 1) * P], ident[:])
                last.then_inc(ps["hT"], 1)

        lead_pe(pe, 3, PG)
        h_pair(0)
        bs[3].wait(pe, "rb_ready", 1)
        fm_pair(pe, PG + 4, 0, GB[4:6], v_hi, v_lo, KD)
        h_pair(1)
        fm_pair(pe, PG + 5, 1, GB[4:6], v_hi, v_lo, KD)
        h_pair(2)
        h_pair(3)
        pe.wait_ge(ps["hT_out"], 4)
        fm_pair(pe, PG + 6, 0, GB[6:8], v_hi, v_lo, KD)

        def y_T(m, tb):
            return nc.tensor.transpose(B[TBANK[m // 4][tb]][:, (m % 4) * P:(m % 4 + 1) * P],
                                       yg[:, m, tb * P:(tb + 1) * P], ident[:])

        fm_pair(pe, PG + 7, 1, GB[6:8], v_hi, v_lo, KD)
        pe.wait_ge(ps["hT_out"], KD)
        for m in range(4):
            pe.wait_ge(ps["yg"], m + 1)
            for tb in range(TB):
                y_T(m, tb)
        pe.wait_ge(ps["g_scaled"], KD)
        for m in range(4, KD):
            if m == KD - 1:
                y_sums_pe(pe, 4, SUMS)
            if m >= 6:
                pe.wait_ge(ps["yg_last"], m - 5)
            else:
                pe.wait_ge(ps["yg"], m + 1)
            for tb in range(3):
                last = y_T(m, tb)
        last.then_inc(ps["y_T"], 1)
        pe.wait_ge(ps["o_out"], 1)
        for m in range(4, KD):
            last = y_T(m, 3)
        last.then_inc(ps["y_T"], 1)

    def gate_dve(dve):
        lead_dve(dve, 3, PG)

        def scale(m):
            dve_after(dve, PG + (2 + m // 2 if m < 4 else 2 * (m // 2) + 1))
            nc.vector.tensor_tensor(ys[:, m, :], B[GB[m]][:], r_b[:], ALU.mult).then_inc(ps["g_scaled"], 1)

        def times_e(m):
            dve.wait_ge(ps["g_sig"], m + 1)
            nc.vector.tensor_tensor(ys[:, m, :], ys[:, m, :], e_sb[:, m, :], ALU.mult).then_inc(ps["gy"], 1)
        for m in range(KD):
            scale(m)
            if m >= 1:
                times_e(m - 1)
        times_e(KD - 1)
        for m in (6, 7):
            dve.wait_ge(ps["gy"], m + 1)
            nc.vector.tensor_scalar(yg[:, m, :], ys[:, m, :], col("ple_post_norm", m), None,
                                    ALU.mult).then_inc(ps["yg_last"], 1)
        bs[4].wait(dve, "y_sum", 1)
        dlink(dve, rsqrt(dve, r1c, B[SUMS][:, 0:TB], TB, 1.0 / D))
        dve.wait_ge(ps["y_T"], 1)
        dve.wait_ge(ps["hT_out"], KD)
        for tb in range(TB):
            for a in range(2):
                if tb == TB - 1 and a == 1:
                    dve.wait_ge(ps["y_T"], 2)
                o = o_sb[:, tb, 512 * a:512 * a + 512]
                nc.vector.scalar_tensor_tensor(o, B[TBANK[a][tb]][:], r1c[:, tb:tb + 1], o, ALU.mult,
                                               ALU.add).then_inc(ps["o_out"], 1)

    def gate_act(act):
        lead_act(act, 3, PG)
        b = bs[4]

        def h_out(g):
            for f in range(2):
                m = 2 * g + f
                act.wait_ge(ps["hT"], m + 1)
                nc.scalar.activation(o_sb[:, :, m * P:(m + 1) * P], v4(B[HB[m]][:]), ACT.Copy).then_inc(ps["hT_out"], 1)

        def squares(p):
            act.wait_ge(ps["gy"], p + 1)
            if p >= 4:
                b.wait(act, "y_acc", p - 3)
            else:
                bs[3].wait(act, "h_acc", KD)
            nc.scalar.activation(scratch[:, p % 4, :], ys[:, p, :], ACT.Square).then_inc(b["ysq_act"], 1)

        def sigmoid(m):
            act.wait_ge(ps["g_scaled"], m + 1)
            nc.scalar.activation(ys[:, m, :], ys[:, m, :], ACT.Sigmoid).then_inc(ps["g_sig"], 1)

        h_out(0)
        for m in range(4):
            sigmoid(m)
            if m >= 1:
                squares(m - 1)
            if m == 1:
                hi_upto(act, PG + 7)
                h_out(1)
        squares(3)
        h_out(2)
        h_out(3)
        for m in range(4, KD):
            sigmoid(m)
            if m >= 5:
                squares(m - 1)
        squares(KD - 1)

    def gate_pool(pool):
        for m in range(6):
            if m >= 1:
                y_squares_pool(pool, 4, m - 1)
            pool.wait_ge(ps["gy"], m + 1)
            nc.gpsimd.tensor_scalar(yg[:, m, :], ys[:, m, :], col("ple_post_norm", m), None, ALU.mult).then_inc(ps["yg"], 1)
        y_squares_pool(pool, 4, 5)

    block = ctx.enter_context(nc.Block())

    @block.sync
    def _(sp):
        sp.dma_start(ident[:], const["ident"]).then_inc(ident_in, 16)
        def load_x(half, landed):
            c = slice(512 * half, 512 * half + 512)
            sp.dma_start(x_tm[:, :, c], w["x"][0, :, c].rearrange("(b p) d -> p b d", p=P)).then_inc(landed, 16)

        load_x(0, x_in)
        r = 0
        for name, rows in VEC_ROWS:
            src = w[name][0]
            src = src.rearrange("j (m p) -> (j m) p", p=P) if name == "ml_conv_w" else src.rearrange("(m p) -> m p", p=P)
            sp.dma_start(vec_rows[r:r + rows, :], src).then_inc(consts_in, 16)
            r += rows
        load_x(1, x_late)
        sp.dma_start(ifb[0:8, 0:1], w["ml_i_bias"].rearrange("a d h -> (d h) a")).then_inc(bias_in, 16)
        sp.dma_start(ifb[0:8, 1:2], w["ml_f_bias"].rearrange("a d h -> (d h) a")).then_inc(bias_in, 16)
        sp.dma_start(trig[:], const["trig"]).then_inc(pos_in, 16)
        sp.dma_start(pos_i[:], w["positions"].broadcast_to([P, S])).then_inc(pos_in, 16)
        f1[0](sp)
        mixer_sp(sp)
        f2[0](sp)
        for i in range(2):
            sp.dma_start(p_tm[i][:], w["p"][0, 0, 256 * i:256 * i + 256].rearrange("(b p) d -> p b d", p=P)).then_inc(p_in, 16)
        for j in range(2):
            cols2(sp, EP + j, w["ple_w_proj"], 0, 512 * j)
        for j in range(8):
            half, g = (j // 2, j % 2) if j < 4 else (j % 2, j // 2)
            cols4(sp, PG + j, w["ple_w_gate"], half, 256 * g)
        for tb in range(TB):
            sp.wait_ge(ps["o_out"], 2 * tb + 2)
            sp.dma_start(out[0, tb * P:(tb + 1) * P, :], o_sb[:, tb, :]).then_inc(out_stored, 16)
        sp.wait_ge(out_stored, 64)

    @block.gpsimd
    def _(pool):
        nc.gpsimd.memset(ones[:], 1.0).then_inc(ones_made, 1)
        h_squares_pool(pool, 0)
        for p in range(ADDED):
            y_squares_pool(pool, 1, p)
        h_squares_pool(pool, 1)
        bs[1].wait(pool, "y_sum", 1)
        plink(pool, nc.gpsimd.memset(maskbig[:], 0.0))
        for d in range(2):
            sgn = 1 if d == 0 else -1
            nc.gpsimd.affine_select(out=maskbig[:, d, :], in_=maskbig[:, d, :], compare_op=ALU.is_ge, fill=BIG, base=0,
                                    pattern=[[sgn, P]], channel_multiplier=-sgn).then_inc(masks_made, 1)
        mixer_pool(pool)
        for p in range(ADDED):
            y_squares_pool(pool, 2, p)
        h_squares_pool(pool, 2)
        for p in range(ADDED):
            y_squares_pool(pool, 3, p)
        h_squares_pool(pool, 3)
        gate_pool(pool)

    @block.vector
    def _(dve):
        b = bs[0]
        for m in range(KD):
            if m == 4:
                dve.wait_ge(vecs_T, 1)
                nc.vector.tensor_copy(cols[:], B[3][:, 0:NVEC]).then_inc(cols_ready, 1)
                dve.wait_ge(cols_ready, 1)
                lo_upto(dve, 0)
                for late in range(m - 1):
                    if late == 2:
                        lo_upto(dve, 1)
                    v_lo_dve(dve, 0, late, gain("ffn1_pre_norm"))
            b.wait(dve, "y_ready", m + 1)
            nc.vector.tensor_copy(h[:, m, :], B[YBANK[m]][:]).then_inc(b["h_ready"], 1)
            if m >= 4:
                v_lo_dve(dve, 0, m - 1, gain("ffn1_pre_norm"))
            if m == 4:
                lo_upto(dve, 2)
        v_lo_dve(dve, 0, KD - 1, gain("ffn1_pre_norm"))
        for a, name in ((0, "ffn1_post_norm"), (8, "ffn2_post_norm")):
            dlink(dve, nc.vector.tensor_scalar(halfpost[:, a:a + 8], cols[:, VEC[name]:VEC[name] + 8], 0.5, None, ALU.mult))
        dve.wait_ge(pos_in, 32)
        dlink(dve, nc.vector.tensor_copy(turns[:], pos_i[:]))
        dlink(dve, nc.vector.tensor_scalar(ang[:], turns[:], trig[:, 0:1], None, ALU.mult))
        dlink(dve, nc.vector.tensor_scalar(turns[:], ang[:], float(1 / (2 * np.pi)), trig[:, 1:2], ALU.mult, ALU.add))
        magic = float(1.5 * 2 ** 23)
        dlink(dve, nc.vector.tensor_scalar(turns[:], turns[:], magic, None, ALU.add))
        dlink(dve, nc.vector.tensor_scalar(turns[:], turns[:], -magic, None, ALU.add))
        for piece in TWO_PI:
            dlink(dve, nc.vector.scalar_tensor_tensor(ang[:], turns[:], -piece, ang[:], ALU.mult, ALU.add))
        dlink(dve, nc.vector.tensor_scalar(CS[:], ang[:], trig[:, 3:4], None, ALU.add))
        lim = float(np.float32(3.1415925))
        nc.vector.tensor_scalar(CS[:], CS[:], lim, -lim, ALU.min, ALU.max).then_inc(ang_ready, 1)
        dve.wait_ge(cs_ready, 1)
        dlink(dve, nc.vector.memset(CS[0:64, :], 1.0))
        f1[2](dve)
        for p in range(1, KD, 2):
            y_tile(1, True, dve, p, f1[4], ybank)
        lo_upto(dve, CQ + 2)
        boundary_dve(dve, 1, half_post(0), gain("mix_pre_norm"))
        mixer_dve(dve)
        for p in range(1, KD, 2):
            y_tile(2, True, dve, p, y_wo(dve_after), ybank)
        boundary_dve(dve, 2, gain("mix_post_norm"), gain("ffn2_pre_norm"))
        f2[2](dve)
        for p in range(1, KD, 2):
            y_tile(3, True, dve, p, f2[4], ybank)
        pT_dve(dve)
        lo_upto(dve, EP + 1)
        bs[3].wait(dve, "y_sum", 1)
        rsqrt(dve, r1c, B[YBANK[0]][:, 0:TB], TB, 1.0 / D).then_inc(bs[3]["r1_ready"], 1)
        lo_upto(dve, EP + 2)
        bs[3].wait(dve, "r1b_ready", 1)
        lo_upto(dve, EP + 3)
        for m in range(KD):
            if m == 4:
                lo_upto(dve, EP + 4)
            h_tile_dve(dve, 3, m, half_post(1))
            if m >= 1:
                v_lo_dve(dve, 3, m - 1, gain("ple_pre_norm"))
        v_lo_dve(dve, 3, KD - 1, gain("ple_pre_norm"))
        gate_dve(dve)

    @block.scalar
    def _(act):
        act.wait_ge(cols_ready, 1)
        hi_upto(act, 0)
        v_tiles_act(act, 0, gain("ffn1_pre_norm"), {2: lambda: hi_upto(act, 1), 4: lambda: hi_upto(act, 2)})
        act.wait_ge(ang_ready, 1)
        nc.scalar.activation(CS[:], CS[:], ACT.Sin, scale=trig[:, 2:3]).then_inc(cs_ready, 1)
        f1[3](act)
        for p in range(0, KD, 2):
            y_tile(1, False, act, p, f1[4], ybank)
        hi_upto(act, CQ + 2)
        v_tiles_act(act, 1, gain("mix_pre_norm"))
        mixer_act(act)
        for p in range(0, KD, 2):
            y_tile(2, False, act, p, y_wo(act_after), ybank)
        hi_upto(act, UP2 + 2)
        v_tiles_act(act, 2, gain("ffn2_pre_norm"))
        f2[3](act)
        for p in range(0, KD, 2):
            y_tile(3, False, act, p, f2[4], ybank)
        pT_act(act)
        e_act(act, 0)
        v_tiles_act(act, 3, gain("ple_pre_norm"), {3: lambda: e_act(act, 1)})
        gate_act(act)

    @block.tensor
    def _(pe):
        pe.wait_ge(ident_in, 16)
        pe.wait_ge(x_in, 16)
        for m in range(KD):
            if m == 4:
                pe.wait_ge(consts_in, 16 * len(VEC_ROWS))
                nc.tensor.transpose(B[3][:, 0:NVEC], vec_rows[0:NVEC, :], ident[0:NVEC, 0:NVEC]).then_inc(vecs_T, 1)
                pe.wait_ge(x_late, 16)
            if m == 7:
                pe.wait_ge(cols_ready, 1)
            for tb in range(TB):
                last = nc.tensor.transpose(B[YBANK[m]][:, tb * P:(tb + 1) * P], x_tm[:, tb, m * P:(m + 1) * P], ident[:])
            last.then_inc(bs[0]["y_ready"], 1)
        pe.wait_ge(ones_made, 1)
        f1[1](pe)
        boundary_pe(pe, 1)
        mixer_pe(pe)
        boundary_pe(pe, 2)
        f2[1](pe)
        boundary_pe(pe, 3)
        gate_pe(pe)



TWO_PI = [6.28125, 0.0019350051879882812, 3.019813448190689e-07, 1.0253131677018246e-11]


def kernel(**inputs):
    import numpy as _np
    import concourse.bacc as _bacc
    from concourse import mybir as _mybir
    from concourse.bass_utils import run_bass_kernel_spmd as _run

    nc = _bacc.Bacc("TRN2", target_bir_lowering=False, num_devices=1)
    arrays, w = {}, {}
    for name, a in inputs.items():
        a = _np.ascontiguousarray(a)
        arrays[f"in_{name}"] = a
        w[name] = nc.dram_tensor(f"in_{name}", a.shape, _mybir.dt.from_np(a.dtype), kind="ExternalInput").ap()
    ident = _np.eye(P, dtype=_np.float32)
    trig = _np.zeros((P, 4), _np.float32)
    freq = (10000.0 ** (-_np.arange(0, ROPE, 2, dtype=_np.float64) / ROPE)).astype(_np.float32)
    trig[64:128, 0] = _np.tile(freq, 4)
    trig[0:96, 1] = 0.25
    trig[:, 2] = 1.0
    trig[96:112, 2] = -1.0
    trig[0:96, 3] = _np.pi / 2
    arrays["ident"], arrays["trig"] = ident, trig
    const = {k: nc.dram_tensor(k, arrays[k].shape, F32, kind="ExternalInput").ap() for k in ("ident", "trig")}
    out = nc.dram_tensor("out", (1, S, D), F32, kind="ExternalOutput").ap()
    program(nc, w, const, out)
    return _run(nc, [arrays], core_ids=[0]).results[0]["out"]
```
